# Optimizing a Trainium2 kernel written in Bass

```python
import jax, jax.numpy as jnp
from jax import lax
import numpy as np

D_MODEL = 2048
BATCH = 1
SEQ = 256
DEPTH = 1

CONF_WIDTH = D_MODEL // 2
CONF_KERNEL = 31
SCONV_WIDTH = D_MODEL // 2
SCONV_KERNEL = 3
HEAD_DIM = 64
N_Q_HEADS = (D_MODEL // 2) // HEAD_DIM
N_KV_HEADS = 4
Q_WIDTH = N_Q_HEADS * HEAD_DIM
KV_WIDTH = N_KV_HEADS * HEAD_DIM
WINDOW = 128
BLOCK = 128
N_BRANCH = 3
D_FF = 4 * D_MODEL
RMS_EPS = 1e-6
LN_EPS = 1e-5
IN_SPLITS = (CONF_WIDTH, CONF_WIDTH,
             SCONV_WIDTH, SCONV_WIDTH, SCONV_WIDTH,
             Q_WIDTH, KV_WIDTH, KV_WIDTH,
             N_BRANCH * D_MODEL)
IN_WIDTH = sum(IN_SPLITS)

kernel_name = "hybrid_conformer_shortconv_swa_sink_block"

def rmsnorm(x, g):
    xf = x.astype(jnp.float32)
    y = xf * lax.rsqrt(jnp.mean(xf * xf, axis=-1, keepdims=True) + RMS_EPS)
    return y.astype(x.dtype) * g

def layernorm(x, g, b):
    xf = x.astype(jnp.float32)
    mu = jnp.mean(xf, axis=-1, keepdims=True)
    var = jnp.mean(jnp.square(xf - mu), axis=-1, keepdims=True)
    y = (xf - mu) * lax.rsqrt(var + LN_EPS)
    return y.astype(x.dtype) * g + b

def causal_depthwise_conv(x, w):
    k, c = w.shape
    return lax.conv_general_dilated(
        x, w[:, None, :].astype(x.dtype), window_strides=(1,),
        padding=((k - 1, 0),), dimension_numbers=("NWC", "WIO", "NWC"),
        feature_group_count=c)

def split_columns(u):
    outs, start = [], 0
    for width in IN_SPLITS:
        outs.append(u[..., start:start + width])
        start += width
    return outs

def sliding_window_sink_attention(q, k, v, sinks):
    b, s, _ = q.shape
    nb = s // BLOCK
    grp = N_Q_HEADS // N_KV_HEADS
    qb = q.reshape(b, nb, BLOCK, N_KV_HEADS, grp, HEAD_DIM)

    def band(t):
        t = t.reshape(b, s, N_KV_HEADS, HEAD_DIM)
        prev = jnp.pad(t, ((0, 0), (BLOCK, 0), (0, 0), (0, 0)))[:, :s]
        prev = prev.reshape(b, nb, BLOCK, N_KV_HEADS, HEAD_DIM)
        cur = t.reshape(b, nb, BLOCK, N_KV_HEADS, HEAD_DIM)
        return jnp.concatenate([prev, cur], axis=2)

    kb, vb = band(k), band(v)
    scores = jnp.einsum("bnqhgd,bnkhd->bnhgqk", qb, kb,
                        preferred_element_type=jnp.float32) * (HEAD_DIM ** -0.5)
    blk = jnp.arange(nb)
    qpos = blk[:, None, None] * BLOCK + jnp.arange(BLOCK)[None, :, None]
    kpos = (blk[:, None, None] - 1) * BLOCK + jnp.arange(2 * BLOCK)[None, None, :]
    diff = qpos - kpos
    valid = (diff >= 0) & (diff < WINDOW) & (kpos >= 0)
    scores = jnp.where(valid[None, :, None, None], scores, -jnp.inf)
    sink = sinks.astype(jnp.float32).reshape(1, 1, N_KV_HEADS, grp, 1, 1)
    m = jnp.maximum(jnp.max(scores, axis=-1, keepdims=True), sink)
    p = jnp.exp(scores - m)
    denom = jnp.sum(p, axis=-1, keepdims=True) + jnp.exp(sink - m)
    probs = (p / denom).astype(v.dtype)
    out = jnp.einsum("bnhgqk,bnkhd->bnqhgd", probs, vb)
    return out.reshape(b, s, Q_WIDTH)

def setup_inputs(seed: int = 0) -> dict:
    key = jax.random.key(seed)
    ks = jax.random.split(key, 20)
    f32 = jnp.float32

    def nrm(k, shape, scale):
        return jax.random.normal(k, shape, f32) * scale

    return {
        "x": nrm(ks[0], (BATCH, SEQ, D_MODEL), 1.0),
        "norm_mix_g": 1.0 + nrm(ks[1], (DEPTH, D_MODEL), 0.02),
        "w_in": nrm(ks[2], (DEPTH, D_MODEL, IN_WIDTH), D_MODEL ** -0.5),
        "gate_b": nrm(ks[3], (DEPTH, N_BRANCH, D_MODEL), 0.02),
        "conf_dw": nrm(ks[4], (DEPTH, CONF_KERNEL, CONF_WIDTH), CONF_KERNEL ** -0.5),
        "conf_ln_g": 1.0 + nrm(ks[5], (DEPTH, CONF_WIDTH), 0.02),
        "conf_ln_b": nrm(ks[6], (DEPTH, CONF_WIDTH), 0.02),
        "w_conf_out": nrm(ks[7], (DEPTH, CONF_WIDTH, D_MODEL), CONF_WIDTH ** -0.5),
        "sconv_w": nrm(ks[8], (DEPTH, SCONV_KERNEL, SCONV_WIDTH), SCONV_KERNEL ** -0.5),
        "w_sconv_out": nrm(ks[9], (DEPTH, SCONV_WIDTH, D_MODEL), SCONV_WIDTH ** -0.5),
        "sinks": nrm(ks[10], (DEPTH, N_Q_HEADS), 0.5),
        "w_attn_out": nrm(ks[11], (DEPTH, Q_WIDTH, D_MODEL), Q_WIDTH ** -0.5),
        "w_mix_out": nrm(ks[12], (DEPTH, D_MODEL, D_MODEL), D_MODEL ** -0.5),
        "norm_ffn_g": 1.0 + nrm(ks[13], (DEPTH, D_MODEL), 0.02),
        "w_up": nrm(ks[14], (DEPTH, D_MODEL, D_FF), D_MODEL ** -0.5),
        "w_down": nrm(ks[15], (DEPTH, D_FF, D_MODEL), D_FF ** -0.5),
        "final_g": 1.0 + nrm(ks[16], (D_MODEL,), 0.02),
    }

def reference(x, norm_mix_g, w_in, gate_b, conf_dw, conf_ln_g, conf_ln_b, w_conf_out,
              sconv_w, w_sconv_out, sinks, w_attn_out, w_mix_out, norm_ffn_g,
              w_up, w_down, final_g):
    b, s, d = x.shape
    for l in range(DEPTH):
        h = rmsnorm(x, norm_mix_g[l])
        u = h @ w_in[l]
        a_val, a_gate, b_gate, c_gate, b_h, q, k, v, g = split_columns(u)

        a = a_val * jax.nn.sigmoid(a_gate)
        a = causal_depthwise_conv(a, conf_dw[l])
        a = jax.nn.silu(layernorm(a, conf_ln_g[l], conf_ln_b[l]))
        y_a = a @ w_conf_out[l]

        sc = causal_depthwise_conv(c_gate * b_h, sconv_w[l])
        y_b = (b_gate * sc) @ w_sconv_out[l]

        y_c = sliding_window_sink_attention(q, k, v, sinks[l]) @ w_attn_out[l]

        gates = jax.nn.sigmoid(g.reshape(b, s, N_BRANCH, d) + gate_b[l])
        merged = gates[:, :, 0] * y_a + gates[:, :, 1] * y_b + gates[:, :, 2] * y_c
        x = x + merged @ w_mix_out[l]

        h = rmsnorm(x, norm_ffn_g[l])
        x = x + jnp.square(jax.nn.relu(h @ w_up[l])) @ w_down[l]
    return rmsnorm(x, final_g)


_drawn_inputs = setup_inputs


def setup_inputs(seed=0):
    import zlib

    import numpy as np

    out = dict(_drawn_inputs(seed))
    spreads = {}
    factors = {'norm_mix_g': 2.852,
     'gate_b': 8.0,
     'conf_ln_g': 60.392,
     'conf_ln_b': 64.0,
     'sinks': 64.0,
     'norm_ffn_g': 11.644,
     'final_g': 8.469}
    for name, (base, spread) in spreads.items():
        noise = np.random.default_rng([zlib.crc32(name.encode()), seed]).standard_normal(out[name].shape)
        drawn = base * np.exp(spread * noise) if base else spread * noise
        out[name] = __import__('jax').numpy.asarray(drawn.astype(out[name].dtype))
    for name, factor in factors.items():
        out[name] = (out[name] * factor).astype(out[name].dtype)
    return out
```

```python
import concourse.bass as bass
from concourse import mybir
from contextlib import ExitStack

F32 = mybir.dt.float32
F32R = mybir.dt.float32r
ACT = mybir.ActivationFunctionType
ALU = mybir.AluOpType
AX = mybir.AxisListType

P = 128
D = 2048
SEQ = 256
FF = 4 * D
NT = D // P
W2 = D // 2
HT = W2 // P
TAPS = 31
TAPS3 = 3
HD = 64
HEADS = W2 // HD
KVH = 4
KVW = KVH * HD
BLK = 128
SC = 3 * BLK
MASKED = -3.0e38
RMS_EPS = 1e-6
LN_EPS = 1e-5

COLS = 256
KT = 4
ROWS = KT * P
RING = 4
LOOKAHEAD = 3
KFULL = D // ROWS
KHALF = W2 // ROWS

C_AVAL, C_AGATE = 0, W2
C_B, C_C, C_BH = 2 * W2, 3 * W2, 4 * W2
C_Q, C_K, C_V = 5 * W2, 6 * W2, 6 * W2 + KVW
C_G = 6 * W2 + 2 * KVW

PR_GB, PR_G1, PR_G2, PR_GF = 0, 48, 64, 80
PR_LNG, PR_LNB, PR_W3, PR_DW = 128, 136, 144, 256
PR_A, PR_B = 96, 40


class Phase:

    def __init__(self, name, trips, groups, slab0, group0):
        self.name, self.trips, self.slab0, self.group0 = name, trips, slab0, group0
        self.slabs = []
        for n, size in enumerate(groups):
            self.slabs += [(n, i, size) for i in range(size)]
        self.ngroups = len(groups)
        self.nslabs = len(self.slabs)
        assert self.nslabs % RING == 0


def plan():
    rows = [("glu", 4, [KFULL] * 2), ("short", 4, [KFULL] * 3), ("kv", 1, [KFULL] * 2),
            ("q", 2, [KFULL] * 2),
            ("B", 4, [KFULL, KHALF] * 2), ("C", 4, [KFULL, KHALF] * 2), ("A", 4, [KFULL, KHALF] * 2),
            ("mix", 4, [KFULL] * 2)]
    phases, s, g = {}, 0, 0
    for name, trips, groups in rows:
        ph = phases[name] = Phase(name, trips, groups, s, g)
        s, g = s + trips * ph.nslabs, g + trips * ph.ngroups
    for name in ("up", "down"):
        ph = phases[name] = Phase(name, 4, [KFULL] * 2, s, g)
        s, g = s + 4 * ph.nslabs, g + 4 * ph.ngroups
    return phases


PH = plan()
CHUNKS = FF // D
CHUNK_SLABS = 2 * 4 * PH["up"].nslabs
CHUNK_GROUPS = 2 * 4 * PH["up"].ngroups
TOTAL = PH["up"].slab0 + CHUNKS * CHUNK_SLABS

CONV_SHORT = dict(enumerate([3, 2, 2, 1, 2, 2, 2, 0, 2, 2, 2, 0]))
CONV_B = {0: 4, 2: 4, 8: 3}
assert sum(CONV_SHORT.values()) + sum(CONV_B.values()) == TAPS


def walk(eng, body):
    def loop(name, c=0, first=0):
        with eng.Fori(first, PH[name].trips) as t:
            body(PH[name], c, t)

    body(PH["glu"], 0, 0)
    loop("glu", first=1)
    loop("short")
    body(PH["kv"], 0, 0)
    for t in range(PH["q"].trips):
        body(PH["q"], 0, t)
    body("v tokens", 0, 0)
    loop("B")
    for t in range(PH["C"].trips):
        body(PH["C"], 0, t)
    loop("A")
    loop("mix")
    body(PH["up"], 0, 0)
    loop("up", first=1)
    loop("down")
    with eng.Fori(1, CHUNKS - 1) as c:
        loop("up", c)
        loop("down", c)
    loop("up", CHUNKS - 1)
    for t in range(PH["down"].trips):
        body(PH["down"], CHUNKS - 1, t)


def slab_of(ph, c, t, k):
    return ph.slab0 + k + t * ph.nslabs + c * CHUNK_SLABS


def group_of(ph, c, t, n):
    return ph.group0 + n + t * ph.ngroups + c * CHUNK_GROUPS


def build(nc, x, norm_mix_g, w_in, gate_b, conf_dw, conf_ln_g, conf_ln_b, w_conf_out, sconv_w,
          w_sconv_out, sinks, w_attn_out, w_mix_out, norm_ffn_g, w_up, w_down, final_g, out):
    w_in, w_conf_out, w_sconv_out = w_in[0], w_conf_out[0], w_sconv_out[0]
    w_attn_out, w_mix_out, w_up, w_down = w_attn_out[0], w_mix_out[0], w_up[0], w_down[0]

    ctx = ExitStack()
    with ctx:
        def sb(name, shape, dt=F32):
            return ctx.enter_context(nc.sbuf_tensor(name, shape, dt))

        def sem(name):
            return ctx.enter_context(nc.semaphore(name))

        w_raw = sb("w_raw", [P, RING, KT, COLS])
        w_hi = sb("w_hi", [P, RING, KT, COLS], F32R)
        w_lo = sb("w_lo", [P, RING, KT, COLS], F32R)
        res = sb("res", [P, NT, SEQ])
        h_hl = sb("h_hl", [P, NT, 2, SEQ], F32R)
        z_ba = sb("z_ba", [P, HT, 2, SEQ], F32R)
        merged = sb("merged", [P, NT, SEQ])
        PADL = TAPS - 1
        GLU_AT = HT * 2 * SEQ
        CONV_AT = GLU_AT + HT * (PADL + SEQ)
        REGION = CONV_AT + HT * SEQ
        region = sb("region", [P, REGION])

        def view(name, whole, offset, shape, dt=F32):
            return nc.alloc_sbuf_tensor_at(name, shape, dt, offset=nc.lookup_mloc(whole).addr + 4 * offset)

        z_c = view("z_c", region, 0, [P, HT, 2, SEQ], F32R)
        glu = view("glu", region, GLU_AT, [P, HT, PADL + SEQ])
        conv = view("conv", region, CONV_AT, [P, HT, SEQ])
        m_hl = view("m_hl", region, 0, [P, NT, 2, SEQ], F32R)
        x_tok = view("x_tok", region, 0, [P, 2, D])
        dw_rows = view("dw_rows", region, GLU_AT, [TAPS, W2])
        y_tok = view("y_tok", merged, 0, [P, 2, D])

        q_t = sb("q_t", [P, HT, SEQ])
        k_dup = sb("k_dup", [P, KVH, SEQ])
        v_tok = sb("v_tok", [P, 2, KVW])
        pair = [sb(f"pair{i}", [P, 2, SEQ]) for i in range(3)]
        gate = sb("gate", [P, 2, SEQ])
        gated = sb("gated", [P, 2, (TAPS3 - 1) + SEQ])
        probs = sb("probs", [P, 2, 2, SC])
        probs_t = sb("probs_t", [P, 2, SC])
        q_now = sb("q_now", [P, 2, SEQ])
        k_now = sb("k_now", [P, 1, SEQ])
        v_now = sb("v_now", [P, 2, P])
        mask = sb("mask", [P, SC])
        ident = sb("ident", [P, P])
        ones = sb("ones", [P, P])
        rstd = sb("rstd", [P, SEQ])
        stat = sb("stat", [P, SEQ])
        rows_a = sb("rows_a", [PR_A, P])
        rows_b = sb("rows_b", [PR_B, P])
        par = sb("par", [P, 512])
        sinkb = sb("sinkb", [P, HEADS])
        top = sb("top", [P, 2, 2, 2])
        neg_top = sb("neg_top", [P, 2, 2, 2])
        sink_d = sb("sink_d", [P, 2, 2, 2])
        sink_e = sb("sink_e", [P, 2, 2, 2])
        denom = sb("denom", [P, 2, 2, 2])
        rdenom = sb("rdenom", [P, 2, 2, 2])
        tok_stat = sb("tok_stat", [P, 4, 2])

        acc = ctx.enter_context(nc.psum_tensor("acc", [P, 8, 512], F32))
        aux = [acc[:, 4 + i, :] for i in range(4)]

        raw_full = [sem(f"raw_full{i}") for i in range(RING)]
        hi_done, lo_done, slab_used, evac_done = sem("hi_done"), sem("lo_done"), sem("slab_used"), sem("evac_done")
        zeroed, consts, par_t, par_ok = sem("zeroed"), sem("consts"), sem("par_t"), sem("par_ok")
        rows_a_in, rows_b_in = sem("rows_a_in"), sem("rows_b_in")
        x_in = [sem(f"x_in{i}") for i in range(4)]
        x_t, x_copied, x_hi, h_lo, x_sq = sem("x_t"), sem("x_copied"), sem("x_hi"), sem("h_lo"), sem("x_sq")
        fold1, stat1, var1, root1, rstd1 = sem("fold1"), sem("stat1"), sem("var1"), sem("root1"), sem("rstd1")
        glu_sig, glu_done, gated_done, short_step, z_b_f, z_b_hi, z_b_lo = (sem(n) for n in (
            "glu_sig", "glu_done", "gated_done", "short_step", "z_b_f", "z_b_hi", "z_b_lo"))
        conv_a, conv_b, conv_c = sem("conv_a"), sem("conv_b"), sem("conv_c")
        k_in, v_t, v_copied = sem("k_in"), sem("v_t"), sem("v_copied")
        q_ready, v_ready, s_ready, masked, top_step, exp_done, norm_step, t_ready, t_copied, o_ready, o_step = (
            sem(n) for n in ("q_ready", "v_ready", "s_ready", "masked", "top_step", "exp_done", "norm_step",
                             "t_ready", "t_copied", "o_ready", "o_step"))
        ln_v, ln_pe, ln_act = sem("ln_v"), sem("ln_pe"), sem("ln_act")
        gate_sig, m_sum, m_hi, m_lo = sem("gate_sig"), sem("m_sum"), sem("m_hi"), sem("m_lo")
        r_hi, r_sq, r_lo, r_sum = sem("r_hi"), sem("r_sq"), sem("r_lo"), sem("r_sum")
        fold2, stat2, var2, root2, rstd2 = sem("fold2"), sem("stat2"), sem("var2"), sem("root2"), sem("rstd2")
        hid_f, hid_hi, hid_lo = sem("hid_f"), sem("hid_hi"), sem("hid_lo")
        y_g, y_sq, y_t, y_copied, y_sum = sem("y_g"), sem("y_sq"), sem("y_t"), sem("y_copied"), sem("y_sum")
        fold3, stat3, var3, root3, rstd3, stored = (sem(n) for n in (
            "fold3", "stat3", "var3", "root3", "rstd3", "stored"))

        scaled = [sem("scaled0"), sem("scaled1")]

        block = ctx.enter_context(nc.Block())

        def both(t2):
            return t2[:, None, :].to_broadcast((P, 2, SEQ))

        def bank(ph, n):
            return 2 * n if ph.ngroups == 3 else 2 * (n % 2)

        @block.sync
        def _(sp):
            def load_x(i):
                cols = slice(i * D // 4, (i + 1) * D // 4)
                sp.dma_start(x_tok[:, :, cols], x[0][:, cols].rearrange("(b p) n -> p b n", p=P)).then_inc(x_in[i], 16)

            def load_slab(ph, c, t, k):
                n, i, _ = ph.slabs[k]
                s = slab_of(ph, c, t, k)
                if ph.name in ("B", "C", "A"):
                    b = {"A": 0, "B": 1, "C": 2}[ph.name]
                    col = t * (2 * COLS) + (n // 2) * COLS
                    if n % 2:
                        w = (w_conf_out, w_sconv_out, w_attn_out)[b]
                    else:
                        w, col = w_in, col + (C_G + b * D)
                    row = i * ROWS
                else:
                    w, starts = {"glu": (w_in, (C_AVAL, C_AGATE)), "short": (w_in, (C_C, C_BH, C_B)),
                                 "kv": (w_in, (C_K, C_V)), "q": (w_in, (C_Q, C_Q + COLS)),
                                 "mix": (w_mix_out, (0, COLS)), "up": (w_up, (0, COLS)),
                                 "down": (w_down, (0, COLS))}[ph.name]
                    step = COLS * (1 if ph.name in ("glu", "short") else 2)
                    col = t * step + starts[n]
                    row = i * ROWS
                    if ph.name == "up":
                        col = c * D + col
                    if ph.name == "down":
                        row = c * D + row
                shared = ph.name in ("B", "A")
                if not (isinstance(s, int) and s < RING or shared and k == 4):
                    sp.wait_ge(lo_done, s + (shared and k == 3) - (RING - 1))
                sp.dma_start(w_raw[:, k % RING], w[bass.ds(row, ROWS), bass.ds(col, COLS)]
                             .rearrange("(a p) n -> p a n", p=P)).then_inc(raw_full[k % RING], 16)

            def trip(ph, c, t):
                if ph == "v tokens":
                    return
                for k in range(ph.nslabs):
                    if ph.name == "glu" and isinstance(t, int) and t == 0 and k == 1:
                        load_x(2)
                        load_x(3)
                        load_dw()
                    if ph.name == "q" and k == 2 and t == 0:
                        sp.wait_ge(evac_done, PH["kv"].group0 + 1)
                        for half in range(2):
                            for odd in range(2):
                                sp.dma_start(k_dup[half * HD:(half + 1) * HD, odd:KVH:2, :],
                                             pair[0][odd * HD:(odd + 1) * HD, :, :]).then_inc(k_in, 16)
                    load_slab(ph, c, t, k)

            def rows(dst, src, done):
                sp.dma_start(dst, src).then_inc(done, 16)

            def load_dw():
                rows(rows_b[0:8, :], conf_ln_g[0].rearrange("(t p) -> t p", p=P), rows_b_in)
                rows(rows_b[8:16, :], conf_ln_b[0].rearrange("(t p) -> t p", p=P), rows_b_in)
                rows(rows_b[16:40, :], sconv_w[0].rearrange("k (t p) -> (k t) p", p=P), rows_b_in)
                rows(dw_rows[:, :], conf_dw[0], rows_b_in)
                rows(sinkb[:, :], sinks.to_broadcast((P, HEADS)), rows_b_in)

            load_x(0)
            rows(rows_a[0:48, :], gate_b[0].rearrange("b (t p) -> (b t) p", p=P), rows_a_in)
            rows(rows_a[48:64, :], norm_mix_g[0].rearrange("(t p) -> t p", p=P), rows_a_in)
            rows(rows_a[64:80, :], norm_ffn_g[0].rearrange("(t p) -> t p", p=P), rows_a_in)
            rows(rows_a[80:96, :], final_g.rearrange("(t p) -> t p", p=P), rows_a_in)
            load_x(1)
            walk(sp, trip)
            for i in range(4):
                b, cols = i % 2, slice((i // 2) * W2, (i // 2 + 1) * W2)
                sp.wait_ge(scaled[b], i // 2 + 1)
                sp.dma_start(out[0][b * P:(b + 1) * P, cols], y_tok[:, b, cols]).then_inc(stored, 16)
            sp.wait_ge(stored, 64)

        @block.gpsimd
        def _(pool):
            pool.memset(ident[:, :], 0.0).then_inc(zeroed, 1)
            pool.memset(ones[:, :], 1.0).then_inc(consts, 1)
            pool.wait_ge(zeroed, 1)
            pool.affine_select(out=ident[:, :], in_=ident[:, :], compare_op=ALU.not_equal, fill=1.0, base=0,
                               pattern=[[-1, P]], channel_multiplier=1).then_inc(consts, 1)
            pool.memset(mask[:, :], 0.0).then_inc(zeroed, 1)
            pool.wait_ge(zeroed, 2)
            for lo in (0, 2 * BLK):
                pool.affine_select(out=mask[:, lo:lo + BLK], in_=mask[:, lo:lo + BLK], compare_op=ALU.is_ge,
                                   fill=MASKED, base=0, pattern=[[-1, BLK]], channel_multiplier=1).then_inc(consts, 1)
            pool.affine_select(out=mask[:, BLK:2 * BLK], in_=mask[:, BLK:2 * BLK], compare_op=ALU.is_ge,
                               fill=MASKED, base=-1, pattern=[[1, BLK]], channel_multiplier=-1).then_inc(consts, 1)

        @block.scalar
        def _(act):
            def hi(ph, c, t, k):
                s = slab_of(ph, c, t, k)
                if isinstance(s, int) and s + LOOKAHEAD >= TOTAL:
                    return
                ahead = k + LOOKAHEAD
                act.wait_ge(raw_full[ahead % RING], 16 * (ph.slab0 // RING + ahead // RING + 1)
                            + t * (16 * ph.nslabs // RING) + c * (16 * CHUNK_SLABS // RING))
                if not (isinstance(s, int) and s == 0):
                    act.wait_ge(slab_used, s)
                act.activation(w_hi[:, ahead % RING], w_raw[:, ahead % RING], ACT.Copy).then_inc(hi_done, 1)

            def start_pair(i):
                act.wait_ge(x_t, i + 1)
                act.activation(res[:, 2 * i:2 * i + 2, :], aux[i % 2][:, :].rearrange("p (e n) -> p e n", e=2),
                               ACT.Copy).then_inc(x_copied, 1)
                act.wait_ge(x_copied, i + 1)
                for e in range(2):
                    act.activation(h_hl[:, 2 * i + e, 0, :], res[:, 2 * i + e, :], ACT.Copy,
                                   scale=par[:, PR_G1 + 2 * i + e:PR_G1 + 2 * i + e + 1]).then_inc(x_hi, 1)
                act.activation(merged[:, 2 * i:2 * i + 2, :], res[:, 2 * i:2 * i + 2, :], ACT.Square).then_inc(x_sq, 1)

            def prologue(s):
                act.wait_ge(raw_full[s], 16)
                act.activation(w_hi[:, s], w_raw[:, s], ACT.Copy).then_inc(hi_done, 1)

            act.wait_ge(par_ok, 1)
            for i in range(4):
                start_pair(i)
            prologue(0)
            for i in range(4, 8):
                start_pair(i)
            prologue(1)
            prologue(2)

            def gates(ph, t, n, b):
                g = group_of(ph, 0, t, n)
                act.wait_ge(evac_done, g + 1)
                for e in range(2):
                    col = t * 4 + (PR_GB + b * NT + n + e)
                    act.activation(gate[:, e, :], pair[0][:, e, :], ACT.Sigmoid,
                                   bias=par[:, bass.ds(col, 1)]).then_inc(gate_sig, 1)

            def exps(t, p):
                act.wait_ge(top_step, t * 10 + 5 * p + 5)
                for e in range(2):
                    for b, cols in ((0, slice(0, BLK)), (1, slice(BLK, SC))):
                        act.activation(probs[:, p, e, cols], probs[:, p, e, cols], ACT.Exp,
                                       bias=neg_top[:, p, e, b:b + 1],
                                       accum_out=denom[:, p, e, b:b + 1]).then_inc(exp_done, 1)
                act.activation(sink_e[:, p], sink_d[:, p], ACT.Exp).then_inc(exp_done, 1)

            def copy_t(t, p):
                act.wait_ge(t_ready, t * 2 + p + 1)
                if p == 1:
                    act.wait_ge(o_ready, t * 2 + 1)
                for e in range(2):
                    act.activation(probs_t[:, e, :], aux[2 + e][:, 0:SC], ACT.Copy).then_inc(t_copied, 1)

            def ln_square():
                act.wait_ge(ln_v, 7)
                for i in range(2):
                    act.activation(glu[:, 4 * i:4 * i + 4, 0:SEQ], conv[:, 4 * i:4 * i + 4, :],
                                   ACT.Square).then_inc(ln_act, 1)

            def ln_root():
                act.wait_ge(ln_v, 12)
                act.activation(stat[:, :], stat[:, :], ACT.Sqrt).then_inc(ln_act, 1)

            def ln_affine(i):
                act.wait_ge(ln_v, 15)
                for j in (2 * i, 2 * i + 1):
                    act.activation(conv[:, j, :], conv[:, j, :], ACT.Identity,
                                   scale=par[:, PR_LNG + j:PR_LNG + j + 1],
                                   bias=par[:, PR_LNB + j:PR_LNB + j + 1]).then_inc(ln_act, 1)

            def ln_sigmoid(i):
                act.wait_ge(ln_act, 3 + 4 * i + 4)
                act.activation(glu[:, 4 * i:4 * i + 4, 0:SEQ], conv[:, 4 * i:4 * i + 4, :],
                               ACT.Sigmoid).then_inc(ln_act, 1)

            def ln_hi(i):
                act.wait_ge(ln_v, 16 + i)
                act.activation(z_ba[:, 4 * i:4 * i + 4, 0, :], conv[:, 4 * i:4 * i + 4, :], ACT.Copy).then_inc(ln_act, 1)

            LN = {22: ln_square, 28: ln_root, 32: lambda: ln_affine(0), 33: lambda: ln_affine(1),
                  34: lambda: (ln_affine(2), ln_affine(3)), 36: lambda: (ln_sigmoid(0), ln_sigmoid(1)),
                  40: lambda: ln_hi(0), 42: lambda: ln_hi(1)}

            def trip(ph, c, t):
                if ph == "v tokens":
                    return
                for k in range(ph.nslabs):
                    hi(ph, c, t, k)
                    n, i, size = ph.slabs[k]
                    ends = i == size - 1
                    g = group_of(ph, c, t, n)
                    if ph.name == "glu":
                        if isinstance(t, int) and t == 0 and k == 2:
                            act.wait_ge(var1, 1)
                            act.activation(rstd[:, :], stat[:, :], ACT.Sqrt).then_inc(root1, 1)
                        if ends and n == 1:
                            act.wait_ge(evac_done, g + 1)
                            act.activation(gate[:, :, :], pair[1][:, :, :], ACT.Sigmoid).then_inc(glu_sig, 1)
                    if ph.name == "short" and ends and n == 2:
                        act.wait_ge(z_b_f, t + 1)
                        act.activation(z_ba[:, bass.ds(t * 2, 2), 0, :], pair[2][:, :, :], ACT.Copy).then_inc(z_b_hi, 1)
                    if ph.name == "B":
                        if k == 0:
                            act.wait_ge(evac_done, PH["q"].group0 + 4)
                            act.activation(q_now[:, :, :], q_t[:, bass.ds(t * 2, 2), :], ACT.Copy,
                                           scale=float(HD) ** -0.5).then_inc(q_ready, 1)
                            act.wait_ge(k_in, 64)
                            act.activation(k_now[:, :, :], k_dup[:, bass.ds(t, 1), :], ACT.Copy).then_inc(q_ready, 1)
                        if k == 2:
                            exps(t, 0)
                        if k == 5:
                            exps(t, 1)
                            copy_t(t, 0)
                        if k == 8:
                            copy_t(t, 1)
                    if ph.name in ("B", "C", "A") and ends and n % 2 == 0:
                        gates(ph, t, n, {"A": 0, "B": 1, "C": 2}[ph.name])
                    if ph.name == "C" and t * ph.nslabs + k in LN:
                        LN[t * ph.nslabs + k]()
                    if ph.name == "A" and ends and n % 2 == 1:
                        j = t * 2 + n // 2
                        act.wait_ge(m_sum, j + 9)
                        act.activation(m_hl[:, bass.ds(j * 2, 2), 0, :], merged[:, bass.ds(j * 2, 2), :],
                                       ACT.Copy).then_inc(m_hi, 1)
                    if ph.name == "mix" and ends:
                        j = t * 2 + n
                        act.wait_ge(evac_done, g + 1)
                        for e in range(2):
                            act.activation(h_hl[:, bass.ds(j * 2 + e, 1), 0, :], res[:, bass.ds(j * 2 + e, 1), :], ACT.Copy,
                                           scale=par[:, bass.ds(j * 2 + (PR_G2 + e), 1)]).then_inc(r_hi, 1)
                        act.activation(pair[n][:, :, :], res[:, bass.ds(j * 2, 2), :], ACT.Square).then_inc(r_sq, 1)
                    if ph.name == "up":
                        if isinstance(t, int) and t == 0 and k == 2:
                            act.wait_ge(var2, 1)
                            act.activation(rstd[:, :], stat[:, :], ACT.Sqrt).then_inc(root2, 1)
                        if ends:
                            j = t * 2 + n
                            act.wait_ge(hid_f, c * 8 + j + 1)
                            act.activation(m_hl[:, bass.ds(j * 2, 2), 0, :], pair[n][:, :, :], ACT.Copy).then_inc(hid_hi, 1)
                    if ph.name == "down" and isinstance(c, int) and c == CHUNKS - 1 and ends:
                        j = 2 * t + n
                        act.wait_ge(evac_done, g + 1)
                        if j >= 2:
                            act.wait_ge(y_t, j - 1)
                        for e in range(2):
                            act.activation(pair[n][:, e, :], res[:, 2 * j + e, :], ACT.Copy,
                                           scale=par[:, PR_GF + 2 * j + e:PR_GF + 2 * j + e + 1]).then_inc(y_g, 1)
                        if j >= 2:
                            act.wait_ge(y_sum, j - 1)
                        act.activation((pair[2], gate)[n][:, :, :], res[:, 2 * j:2 * j + 2, :], ACT.Square).then_inc(y_sq, 1)

            walk(act, trip)
            act.wait_ge(var3, 1)
            act.activation(tok_stat[:, 1, :], tok_stat[:, 0, :], ACT.Sqrt).then_inc(root3, 1)
            act.wait_ge(rstd3, 1)
            act.wait_ge(y_copied, 8)
            for i in range(2):
                act.activation(y_tok[:, 1, i * W2:(i + 1) * W2], y_tok[:, 1, i * W2:(i + 1) * W2], ACT.Copy,
                               scale=tok_stat[:, 2, 1:2]).then_inc(scaled[1], 1)

        @block.vector
        def _(dve):
            def lo(ph, c, t, k):
                s = slab_of(ph, c, t, k)
                if isinstance(s, int) and s + LOOKAHEAD >= TOTAL:
                    return
                q = (k + LOOKAHEAD) % RING
                dve.wait_ge(hi_done, s + (LOOKAHEAD + 1))
                dve.tensor_tensor(w_lo[:, q], w_raw[:, q], w_hi[:, q].bitcast(F32), ALU.subtract).then_inc(lo_done, 1)

            def prologue(s):
                dve.wait_ge(hi_done, s + 1)
                dve.tensor_tensor(w_lo[:, s], w_raw[:, s], w_hi[:, s].bitcast(F32), ALU.subtract).then_inc(lo_done, 1)

            def start_pair(i):
                for e in range(2):
                    dve.wait_ge(x_hi, 2 * i + e + 1)
                    dve.scalar_tensor_tensor(h_hl[:, 2 * i + e, 1, :], res[:, 2 * i + e, :],
                                             par[:, PR_G1 + 2 * i + e:PR_G1 + 2 * i + e + 1],
                                             h_hl[:, 2 * i + e, 0, :].bitcast(F32),
                                             ALU.mult, ALU.subtract).then_inc(h_lo, 1)

            dve.wait_ge(par_t, 1)
            dve.tensor_copy(par[:, 0:PR_A], aux[3][:, 0:PR_A]).then_inc(par_ok, 1)
            dve.wait_ge(par_ok, 1)
            for i in range(4):
                start_pair(i)
            prologue(0)
            for i in range(4, 8):
                start_pair(i)
            prologue(1)
            prologue(2)
            dve.memset(gated[:, :, 0:TAPS3 - 1], 0.0).then_inc(par_ok, 1)
            dve.wait_ge(par_t, 2)
            dve.tensor_copy(par[:, PR_LNG:PR_LNG + PR_B], aux[3][:, PR_LNG:PR_LNG + PR_B]).then_inc(par_ok, 1)
            dve.tensor_copy(par[:, PR_DW:PR_DW + HT * TAPS], aux[3][:, PR_DW:PR_DW + HT * TAPS]).then_inc(par_ok, 1)
            dve.memset(glu[:, :, 0:PADL], 0.0).then_inc(par_ok, 1)
            dve.wait_ge(x_sq, 8)
            for n, w in enumerate((8, 4, 2, 1)):
                if n:
                    dve.wait_ge(fold1, n)
                dve.tensor_tensor(merged[:, 0:w, :], merged[:, 0:w, :], merged[:, w:2 * w, :], ALU.add).then_inc(fold1, 1)

            def mean_eps(dst, src, scale, eps, done):
                dve.tensor_scalar(dst, src, scale, eps, ALU.mult, ALU.add).then_inc(done, 1)

            def tap(tile, k, step, at):
                w = par[:, bass.ds(tile * TAPS + (PR_DW + k), 1)]
                src = glu[:, bass.ds(tile, 1), k:k + SEQ]
                dst = conv[:, bass.ds(tile, 1), :]
                if k == 0:
                    dve.tensor_scalar(dst, src, w, None, ALU.mult).then_inc(step, 1)
                else:
                    if at is not None:
                        dve.wait_ge(step, at)
                    dve.scalar_tensor_tensor(dst, src, w, dst, ALU.mult, ALU.add).then_inc(step, 1)

            def top_of(t, p):
                dve.wait_ge(s_ready, t * 2 + p + 1)
                for e in range(2):
                    dve.tensor_tensor(probs[:, p, e, :], aux[e][:, 0:SC], mask[:, :], ALU.add).then_inc(masked, 1)
                dve.wait_ge(masked, t * 4 + 2 * p + 2)
                dve.reduce_max(top[:, p, :, 0], probs[:, p, :, 0:BLK], AX.X).then_inc(top_step, 1)
                dve.reduce_max(top[:, p, :, 1], probs[:, p, :, BLK:SC], AX.X).then_inc(top_step, 1)
                dve.wait_ge(top_step, t * 10 + 5 * p + 2)
                sink = sinkb[:, bass.ds(t * 4 + 2 * p, 2)][:, :, None].to_broadcast((P, 2, 2))
                dve.tensor_tensor(top[:, p], top[:, p], sink, ALU.max).then_inc(top_step, 1)
                dve.wait_ge(top_step, t * 10 + 5 * p + 3)
                dve.tensor_scalar(neg_top[:, p], top[:, p], -1.0, None, ALU.mult).then_inc(top_step, 1)
                dve.tensor_tensor(sink_d[:, p], sink, top[:, p], ALU.subtract).then_inc(top_step, 1)

            def normalise(t, p):
                dve.wait_ge(exp_done, t * 10 + 5 * p + 5)
                dve.tensor_tensor(denom[:, p], denom[:, p], sink_e[:, p], ALU.add).then_inc(norm_step, 1)
                dve.wait_ge(norm_step, t * 12 + 6 * p + 1)
                dve.reciprocal(rdenom[:, p], denom[:, p]).then_inc(norm_step, 1)
                dve.wait_ge(norm_step, t * 12 + 6 * p + 2)
                for e in range(2):
                    for b, cols in ((0, slice(0, BLK)), (1, slice(BLK, SC))):
                        dve.tensor_scalar(probs[:, p, e, cols], probs[:, p, e, cols], rdenom[:, p, e, b:b + 1], None,
                                          ALU.mult).then_inc(norm_step, 1)

            def head_out(t, p):
                dve.wait_ge(o_ready, t * 2 + p + 1)
                j = t * 2 + p
                for e in range(2):
                    part = slice(e * HD, (e + 1) * HD)
                    dve.tensor_copy(z_c[part, bass.ds(j, 1), 0, :], aux[p][part, None, e * SEQ:(e + 1) * SEQ]).then_inc(o_step, 1)
                dve.wait_ge(o_step, t * 8 + 4 * p + 2)
                for e in range(2):
                    part = slice(e * HD, (e + 1) * HD)
                    dve.tensor_tensor(z_c[part, bass.ds(j, 1), 1, :], aux[p][part, None, e * SEQ:(e + 1) * SEQ],
                                      z_c[part, bass.ds(j, 1), 0, :].bitcast(F32), ALU.subtract).then_inc(o_step, 1)

            def ln_fold(src, base):
                for n, (dst, a, b) in enumerate((
                        (pair[2][:, :, :], src(0, 2), src(2, 4)), (pair[1][:, :, :], src(4, 6), src(6, 8)),
                        (pair[2][:, :, :], pair[2][:, :, :], pair[1][:, :, :]),
                        (stat[:, :], pair[2][:, 0, :], pair[2][:, 1, :]))):
                    if n >= 2:
                        dve.wait_ge(ln_v, base + n)
                    dve.tensor_tensor(dst, a, b, ALU.add).then_inc(ln_v, 1)

            def ln_sum():
                dve.wait_ge(conv_b, 4 * 11)
                dve.wait_ge(conv_c, 4 * TAPS)
                dve.wait_ge(m_sum, 3)
                ln_fold(lambda a, b: conv[:, a:b, :], 0)

            def ln_center():
                dve.wait_ge(ln_pe, 1)
                mean_eps(stat[:, :], aux[2][:, 0:SEQ], 1.0 / W2, 0.0, ln_v)
                dve.wait_ge(ln_v, 5)
                for i in range(2):
                    dve.tensor_tensor(conv[:, 4 * i:4 * i + 4, :], conv[:, 4 * i:4 * i + 4, :],
                                      stat[:, None, :].to_broadcast((P, 4, SEQ)), ALU.subtract).then_inc(ln_v, 1)

            def ln_sum2():
                dve.wait_ge(ln_act, 2)
                dve.wait_ge(m_sum, 4)
                ln_fold(lambda a, b: glu[:, a:b, 0:SEQ], 7)

            def ln_var():
                dve.wait_ge(ln_pe, 2)
                mean_eps(stat[:, :], aux[2][:, 0:SEQ], 1.0 / W2, LN_EPS, ln_v)

            def ln_rstd():
                dve.wait_ge(ln_act, 3)
                dve.reciprocal(stat[:, :], stat[:, :]).then_inc(ln_v, 1)
                dve.wait_ge(ln_v, 13)
                for i in range(2):
                    dve.tensor_tensor(conv[:, 4 * i:4 * i + 4, :], conv[:, 4 * i:4 * i + 4, :],
                                      stat[:, None, :].to_broadcast((P, 4, SEQ)), ALU.mult).then_inc(ln_v, 1)

            def ln_silu(i):
                dve.wait_ge(ln_act, 12 + i)
                dve.tensor_tensor(conv[:, 4 * i:4 * i + 4, :], conv[:, 4 * i:4 * i + 4, :],
                                  glu[:, 4 * i:4 * i + 4, 0:SEQ], ALU.mult).then_inc(ln_v, 1)

            def ln_lo(i):
                dve.wait_ge(ln_act, 14 + i)
                dve.tensor_tensor(z_ba[:, 4 * i:4 * i + 4, 1, :], conv[:, 4 * i:4 * i + 4, :],
                                  z_ba[:, 4 * i:4 * i + 4, 0, :].bitcast(F32), ALU.subtract).then_inc(ln_v, 1)

            LN = {18: ln_sum, 21: ln_center, 24: ln_sum2, 27: ln_var, 30: ln_rstd, 38: lambda: ln_silu(0),
                  39: lambda: ln_silu(1), 42: lambda: ln_lo(0), 44: lambda: ln_lo(1)}

            taps_c = [(tile0 + e, k) for tile0 in (4, 6) for k in range(TAPS) for e in range(2)]
            done_c = [0]

            def taps_static(n):
                for tile, k in taps_c[done_c[0]:done_c[0] + n]:
                    tap(tile, k, conv_c, done_c[0] - 1)
                    done_c[0] += 1

            def trip(ph, c, t):
                if ph == "v tokens":
                    dve.wait_ge(v_t, 1)
                    dve.tensor_copy(v_tok[:, :, :].rearrange("p b n -> p (b n)"), aux[2][:, :]).then_inc(v_copied, 1)
                    return
                for k in range(ph.nslabs):
                    lo(ph, c, t, k)
                    n, i, size = ph.slabs[k]
                    s, g, ends = slab_of(ph, c, t, k), group_of(ph, c, t, n), i == size - 1
                    if ph.name == "glu" and isinstance(t, int) and t == 0:
                        if k == 1:
                            dve.wait_ge(stat1, 1)
                            mean_eps(stat[:, :], aux[2][:, 0:SEQ], 1.0 / D, RMS_EPS, var1)
                        if k == 2:
                            dve.wait_ge(root1, 1)
                            dve.reciprocal(rstd[:, :], rstd[:, :]).then_inc(rstd1, 1)
                            dve.wait_ge(rstd1, 1)
                    if ph.name == "up" and isinstance(t, int) and t == 0:
                        if k == 0:
                            dve.wait_ge(r_sum, 9)
                            dve.tensor_tensor(stat[:, :], pair[2][:, 0, :], pair[2][:, 1, :], ALU.add).then_inc(fold2, 1)
                        if k == 1:
                            dve.wait_ge(stat2, 1)
                            mean_eps(stat[:, :], aux[2][:, 0:SEQ], 1.0 / D, RMS_EPS, var2)
                        if k == 2:
                            dve.wait_ge(root2, 1)
                            dve.reciprocal(rstd[:, :], rstd[:, :]).then_inc(rstd2, 1)
                            dve.wait_ge(rstd2, 1)
                    if ph.name == "short":
                        if k == 0:
                            dve.wait_ge(glu_done, 4)
                            dve.wait_ge(par_ok, 5)
                        first = sum(CONV_SHORT[m] for m in range(k))
                        for m in range(first, first + CONV_SHORT[k]):
                            tap(t, m, conv_a, t * 20 + m)
                        if k in (8, 9, 10):
                            m = k - 8
                            for e in range(2):
                                src = gated[:, e, m:m + SEQ]
                                w = par[:, bass.ds(t * 2 + (PR_W3 + m * HT + e), 1)]
                                if m == 0:
                                    dve.wait_ge(gated_done, t + 1)
                                    dve.tensor_scalar(pair[1][:, e, :], src, w, None, ALU.mult).then_inc(short_step, 1)
                                else:
                                    dve.wait_ge(short_step, t * 6 + (2 * (m - 1) + e + 1))
                                    dve.scalar_tensor_tensor(pair[1][:, e, :], src, w, pair[1][:, e, :], ALU.mult,
                                                             ALU.add).then_inc(short_step, 1)
                    if ph.name == "q":
                        taps_static(4 if not ends else 2)
                    if ph.name == "B":
                        if k == 0:
                            dve.wait_ge(v_copied, 1)
                            dve.wait_ge(consts, 5)
                            for half in range(2):
                                dve.tensor_copy(v_now[:, :, half * HD:(half + 1) * HD],
                                                v_tok[:, :, bass.ds(t * HD, HD)]).then_inc(v_ready, 1)
                        if k in CONV_B:
                            first = 20 + sum(CONV_B[m] for m in CONV_B if m < k)
                            for m in range(first, first + CONV_B[k]):
                                if m == 20:
                                    dve.wait_ge(conv_a, 80)
                                tap(t, m, conv_b, None if m == 20 else t * 11 + (m - 20))
                        if k in (1, 4):
                            top_of(t, k // 4)
                        if k in (3, 6):
                            normalise(t, k // 6)
                        if k in (7, 10):
                            head_out(t, k // 10)
                    if ph.name == "C":
                        at = t * ph.nslabs + k
                        if at < 16:
                            taps_static(5 if not ends else 4)
                        if at == 17:
                            taps_static(len(taps_c))
                        if at in LN:
                            LN[at]()
                    if not ends:
                        continue
                    dve.wait_ge(slab_used, s + 1)
                    a = acc[:, bank(ph, n):bank(ph, n) + 2, 0:SEQ]
                    if ph.name in ("glu", "kv"):
                        dve.tensor_tensor(pair[n][:, :, :], a, both(rstd), ALU.mult).then_inc(evac_done, 1)
                        if ph.name == "glu" and n == 1:
                            dve.wait_ge(glu_sig, t + 1)
                            dve.tensor_tensor(glu[:, bass.ds(t * 2, 2), PADL:PADL + SEQ], pair[0][:, :, :],
                                              gate[:, :, :], ALU.mult).then_inc(glu_done, 1)
                    elif ph.name == "short":
                        dve.tensor_tensor(pair[n][:, :, :], a, both(rstd), ALU.mult).then_inc(evac_done, 1)
                        dve.wait_ge(evac_done, g + 1)
                        if n == 1:
                            dve.tensor_tensor(gated[:, :, TAPS3 - 1:], pair[0][:, :, :], pair[1][:, :, :],
                                              ALU.mult).then_inc(gated_done, 1)
                        if n == 2:
                            dve.wait_ge(short_step, t * 6 + 6)
                            dve.tensor_tensor(pair[2][:, :, :], pair[2][:, :, :], pair[1][:, :, :], ALU.mult).then_inc(z_b_f, 1)
                            dve.wait_ge(z_b_hi, t + 1)
                            dve.tensor_tensor(z_ba[:, bass.ds(t * 2, 2), 1, :], pair[2][:, :, :],
                                              z_ba[:, bass.ds(t * 2, 2), 0, :].bitcast(F32), ALU.subtract).then_inc(z_b_lo, 1)
                    elif ph.name == "q":
                        j = t * 2 + n
                        dve.tensor_tensor(q_t[:, 2 * j:2 * j + 2, :], a, both(rstd), ALU.mult).then_inc(evac_done, 1)
                    elif ph.name in ("B", "C", "A") and n % 2 == 0:
                        dve.tensor_tensor(pair[0][:, :, :], a, both(rstd), ALU.mult).then_inc(evac_done, 1)
                    elif ph.name in ("B", "C", "A"):
                        j = t * 2 + n // 2
                        first = {"B": 0, "C": 16, "A": 32}[ph.name]
                        dve.wait_ge(gate_sig, j * 2 + (first + 2))
                        m = merged[:, bass.ds(j * 2, 2), :]
                        if ph.name == "B":
                            dve.tensor_tensor(m, a, gate[:, :, :], ALU.mult).then_inc(evac_done, 1)
                        else:
                            dve.tensor_tensor(pair[1][:, :, :], a, gate[:, :, :], ALU.mult).then_inc(evac_done, 1)
                            dve.wait_ge(evac_done, g + 1)
                            dve.tensor_tensor(m, m, pair[1][:, :, :], ALU.add).then_inc(m_sum, 1)
                        if ph.name == "A":
                            dve.wait_ge(m_hi, j + 1)
                            dve.tensor_tensor(m_hl[:, bass.ds(j * 2, 2), 1, :], m,
                                              m_hl[:, bass.ds(j * 2, 2), 0, :].bitcast(F32), ALU.subtract).then_inc(m_lo, 1)
                    elif ph.name == "mix":
                        j = t * 2 + n
                        r = res[:, bass.ds(j * 2, 2), :]
                        dve.tensor_tensor(r, a, r, ALU.add).then_inc(evac_done, 1)
                        for e in range(2):
                            dve.wait_ge(r_hi, j * 2 + (e + 1))
                            dve.scalar_tensor_tensor(h_hl[:, bass.ds(j * 2 + e, 1), 1, :], res[:, bass.ds(j * 2 + e, 1), :],
                                                     par[:, bass.ds(j * 2 + (PR_G2 + e), 1)],
                                                     h_hl[:, bass.ds(j * 2 + e, 1), 0, :].bitcast(F32),
                                                     ALU.mult, ALU.subtract).then_inc(r_lo, 1)
                        dve.wait_ge(r_sq, j + 1)
                        dve.wait_ge(r_sum, j + 1)
                        dve.tensor_tensor(pair[2][:, :, :], pair[2][:, :, :], pair[n][:, :, :], ALU.add).then_inc(r_sum, 1)
                    elif ph.name == "up":
                        j = t * 2 + n
                        dve.tensor_tensor(pair[n][:, :, :], a, both(rstd), ALU.mult).then_inc(evac_done, 1)
                        dve.wait_ge(evac_done, g + 1)
                        dve.scalar_tensor_tensor(pair[n][:, :, :], pair[n][:, :, :], 0.0, pair[n][:, :, :], ALU.max,
                                                 ALU.mult).then_inc(hid_f, 1)
                        dve.wait_ge(hid_hi, c * 8 + j + 1)
                        dve.tensor_tensor(m_hl[:, bass.ds(j * 2, 2), 1, :], pair[n][:, :, :],
                                          m_hl[:, bass.ds(j * 2, 2), 0, :].bitcast(F32), ALU.subtract).then_inc(hid_lo, 1)
                    else:
                        j = t * 2 + n
                        r = res[:, bass.ds(j * 2, 2), :]
                        dve.tensor_tensor(r, a, r, ALU.add).then_inc(evac_done, 1)
                        if isinstance(c, int) and c == CHUNKS - 1:
                            finish_pair(j)
                if ph.name == "C" and t == PH["C"].trips - 1:
                    dve.memset(pair[2][:, :, :], 0.0).then_inc(r_sum, 1)

            def finish_pair(j):
                n = j % 2
                dve.wait_ge(y_sq, j + 1)
                src = (pair[2], gate)[n]
                if j == 0:
                    dve.tensor_copy(q_now[:, :, :], src[:, :, :]).then_inc(y_sum, 1)
                else:
                    dve.wait_ge(y_sum, j)
                    dve.tensor_tensor(q_now[:, :, :], q_now[:, :, :], src[:, :, :], ALU.add).then_inc(y_sum, 1)
                if j:
                    copy_y(j - 1)

            def copy_y(j):
                dve.wait_ge(y_t, j + 1)
                dve.tensor_copy(y_tok[:, :, 2 * j * P:(2 * j + 2) * P],
                                aux[j % 2][:, :].rearrange("p (b n) -> p b n", b=2)).then_inc(y_copied, 1)

            walk(dve, trip)
            dve.wait_ge(y_sum, 8)
            dve.tensor_tensor(stat[:, :], q_now[:, 0, :], q_now[:, 1, :], ALU.add).then_inc(fold3, 1)
            copy_y(7)
            dve.wait_ge(stat3, 1)
            mean_eps(tok_stat[:, 0, :], aux[2][:, 0:2], 1.0 / D, RMS_EPS, var3)
            dve.wait_ge(root3, 1)
            dve.reciprocal(tok_stat[:, 2, :], tok_stat[:, 1, :]).then_inc(rstd3, 1)
            dve.wait_ge(rstd3, 1)
            dve.wait_ge(y_copied, 8)
            for i in range(2):
                dve.tensor_scalar(y_tok[:, 0, i * W2:(i + 1) * W2], y_tok[:, 0, i * W2:(i + 1) * W2],
                                  tok_stat[:, 2, 0:1], None, ALU.mult).then_inc(scaled[0], 1)

        @block.tensor
        def _(pe):
            def products(ph, c, t, k, act_hl):
                n, i, size = ph.slabs[k]
                s, g, q = slab_of(ph, c, t, k), group_of(ph, c, t, n), k % RING
                pe.wait_ge(lo_done, s + 1)
                if i == 0 and not (isinstance(g, int) and g < 2):
                    pe.wait_ge(evac_done, g - 1)
                b = bank(ph, n)
                for a in range(KT):
                    kt = i * KT + a
                    first, final = kt == 0, kt == size * KT - 1
                    for m in range(2):
                        dst = acc[:, b + m, 0:SEQ]
                        w_h, w_l = (w[:, q, a, m * P:(m + 1) * P] for w in (w_hi, w_lo))
                        pe.matmul(dst, w_h, act_hl[:, kt, 0, :], start=first, stop=False)
                        pe.matmul(dst, w_h, act_hl[:, kt, 1, :], start=False, stop=False)
                        last = pe.matmul(dst, w_l, act_hl[:, kt, 0, :], start=False, stop=final)
                last.then_inc(slab_used, 1)

            def transposed(dst, src):
                return pe.transpose(dst, src, ident[0:src.shape[0], 0:src.shape[0]])

            def sum_over_partitions(src_done, value, done):
                pe.wait_ge(src_done, value)
                pe.matmul(aux[2][:, 0:SEQ], ones[:, :], stat[:, :] if src_done is not fold1 else merged[:, 0, :],
                          start=True, stop=True).then_inc(done, 1)

            pe.wait_ge(consts, 2)
            pe.wait_ge(rows_a_in, 64)
            transposed(aux[3][:, 0:PR_A], rows_a[:, :]).then_inc(par_t, 1)
            for i in range(8):
                if i % 2 == 0:
                    pe.wait_ge(x_in[i // 2], 16)
                if i >= 2:
                    pe.wait_ge(x_copied, i - 1)
                for e in range(2):
                    for b in range(2):
                        last = transposed(aux[i % 2][:, e * SEQ + b * P:e * SEQ + (b + 1) * P],
                                          x_tok[:, b, (2 * i + e) * P:(2 * i + e + 1) * P])
                last.then_inc(x_t, 1)
            pe.wait_ge(rows_b_in, 5 * 16)
            transposed(aux[3][:, PR_LNG:PR_LNG + PR_B], rows_b[:, :])
            for j in range(HT):
                at = PR_DW + j * TAPS
                last = transposed(aux[3][:, at:at + TAPS], dw_rows[:, j * P:(j + 1) * P])
            last.then_inc(par_t, 1)

            def scores(t, p):
                if p == 0:
                    pe.wait_ge(q_ready, t * 2 + 2)
                    pe.wait_ge(v_ready, t * 2 + 2)
                else:
                    pe.wait_ge(masked, t * 4 + 2)
                for e in range(2):
                    part = slice(e * HD, (e + 1) * HD)
                    for b, cols in ((0, slice(0, BLK)), (1, slice(BLK, SC))):
                        last = pe.matmul(aux[e][:, cols], q_now[part, p, b * BLK:(b + 1) * BLK],
                                         k_now[part, 0, 0:(b + 1) * BLK],
                                         start=True, stop=True)
                last.then_inc(s_ready, 1)

            def transposes(t, p):
                pe.wait_ge(norm_step, t * 12 + 6 * p + 6)
                for e in range(2):
                    for b in range(3):
                        cols = slice(b * BLK, (b + 1) * BLK)
                        last = transposed(aux[2 + e][:, cols], probs[:, p, e, cols])
                last.then_inc(t_ready, 1)

            def values(t, p):
                pe.wait_ge(t_copied, t * 4 + 2 * p + 2)
                for e in range(2):
                    at = e * SEQ
                    pe.matmul(aux[p][:, at:at + BLK], v_now[:, 0, :], probs_t[:, e, 0:BLK], start=True, stop=True)
                    pe.matmul(aux[p][:, at + BLK:at + SEQ], v_now[:, 0, :], probs_t[:, e, BLK:2 * BLK], start=True, stop=False)
                    last = pe.matmul(aux[p][:, at + BLK:at + SEQ], v_now[:, 1, :], probs_t[:, e, 2 * BLK:], start=False, stop=True)
                last.then_inc(o_ready, 1)

            OPERAND = {"B": z_ba, "C": z_c, "A": z_ba, "mix": m_hl, "down": m_hl}

            def trip(ph, c, t):
                if ph == "v tokens":
                    pe.wait_ge(evac_done, PH["kv"].group0 + 2)
                    for b in range(2):
                        for e in range(2):
                            last = transposed(aux[2][:, b * KVW + e * P:b * KVW + (e + 1) * P],
                                              pair[1][:, e, b * P:(b + 1) * P])
                    last.then_inc(v_t, 1)
                    return
                for k in range(ph.nslabs):
                    n, i, size = ph.slabs[k]
                    operand = h_hl
                    if ph.name == "glu" and isinstance(t, int) and t == 0:
                        if n == 0:
                            pe.wait_ge(h_lo, KT * (i + 1))
                        if k == 2:
                            sum_over_partitions(fold1, 4, stat1)
                    if ph.name == "B":
                        if k in (1, 3):
                            scores(t, k // 3)
                        if k in (5, 8):
                            transposes(t, k // 8)
                        if k in (7, 10):
                            values(t, k // 10)
                    if ph.name in ("B", "C", "A") and n % 2:
                        operand = OPERAND[ph.name]
                        if ph.name == "B":
                            pe.wait_ge(z_b_lo, 4)
                        elif ph.name == "C":
                            pe.wait_ge(o_step, 32)
                        else:
                            pe.wait_ge(ln_v, 19)
                    if ph.name == "C" and t * ph.nslabs + k == 20:
                        sum_over_partitions(ln_v, 4, ln_pe)
                    if ph.name == "C" and t * ph.nslabs + k == 26:
                        sum_over_partitions(ln_v, 11, ln_pe)
                    if ph.name == "mix":
                        operand = m_hl
                        pe.wait_ge(m_lo, 2 * (i + 1))
                    if ph.name == "up":
                        pe.wait_ge(r_lo, KT * (i + 1))
                        if isinstance(t, int) and t == 0 and k == 2:
                            sum_over_partitions(fold2, 1, stat2)
                    if ph.name == "down":
                        operand = m_hl
                        pe.wait_ge(hid_lo, c * 8 + 2 * (i + 1))
                        if isinstance(c, int) and c == CHUNKS - 1 and i == 2 and 2 * t + n >= 1:
                            transpose_y(2 * t + n - 1)
                    products(ph, c, t, k, operand)

            def transpose_y(j):
                pe.wait_ge(y_g, 2 * j + 2)
                if j >= 2:
                    pe.wait_ge(y_copied, j - 1)
                for e in range(2):
                    for b in range(2):
                        last = transposed(aux[j % 2][:, b * 2 * P + e * P:b * 2 * P + (e + 1) * P],
                                          pair[j % 2][:, e, b * P:(b + 1) * P])
                last.then_inc(y_t, 1)

            walk(pe, trip)
            transpose_y(7)
            pe.wait_ge(fold3, 1)
            for b in range(2):
                last = pe.matmul(aux[2][:, b:b + 1], stat[:, b * P:(b + 1) * P], ones[:, 0:1], start=True, stop=True)
            last.then_inc(stat3, 1)


_INS = ["x", "norm_mix_g", "w_in", "gate_b", "conf_dw", "conf_ln_g", "conf_ln_b", "w_conf_out", "sconv_w",
        "w_sconv_out", "sinks", "w_attn_out", "w_mix_out", "norm_ffn_g", "w_up", "w_down", "final_g"]


def kernel(**inputs):
    import numpy as np
    import concourse.bacc as bacc
    from concourse.bass_utils import run_bass_kernel_spmd

    nc = bacc.Bacc("TRN2", target_bir_lowering=False, num_devices=1)
    arrays, args = {}, []
    for name in _INS:
        a = np.ascontiguousarray(inputs[name])
        arrays[f"in_{name}"] = a
        args.append(nc.dram_tensor(f"in_{name}", a.shape, mybir.dt.from_np(a.dtype), kind="ExternalInput").ap())
    args.append(nc.dram_tensor("out_y", (1, SEQ, D), F32, kind="ExternalOutput").ap())
    build(nc, *args)
    r = run_bass_kernel_spmd(nc, [arrays], core_ids=[0])
    return r.results[0]["out_y"]
```

```python
import concourse.bass as bass
from concourse import mybir
from contextlib import ExitStack

F32 = mybir.dt.float32
F32R = mybir.dt.float32r
ACT = mybir.ActivationFunctionType
ALU = mybir.AluOpType
AX = mybir.AxisListType

P = 128
D = 2048
SEQ = 256
FF = 4 * D
NT = D // P
W2 = D // 2
HT = W2 // P
TAPS = 31
TAPS3 = 3
HD = 64
HEADS = W2 // HD
KVH = 4
KVW = KVH * HD
BLK = 128
SC = 3 * BLK
MASKED = -3.0e38
RMS_EPS = 1e-6
LN_EPS = 1e-5

COLS = 256
KT = 4
ROWS = KT * P
RING = 4
LOOKAHEAD = 3
KFULL = D // ROWS
KHALF = W2 // ROWS

C_AVAL, C_AGATE = 0, W2
C_B, C_C, C_BH = 2 * W2, 3 * W2, 4 * W2
C_Q, C_K, C_V = 5 * W2, 6 * W2, 6 * W2 + KVW
C_G = 6 * W2 + 2 * KVW

PR_GB, PR_G2, PR_GF, PR_G1 = 0, 48, 64, 80
PR_LNG, PR_LNB, PR_W3, PR_DW = 128, 136, 144, 256
PR_A, PR_B = 80, 40


class Phase:

    def __init__(self, name, trips, groups, slab0, group0):
        self.name, self.trips, self.slab0, self.group0 = name, trips, slab0, group0
        self.slabs = []
        for n, size in enumerate(groups):
            self.slabs += [(n, i, size) for i in range(size)]
        self.ngroups = len(groups)
        self.nslabs = len(self.slabs)
        assert self.nslabs % RING == 0


def plan():
    rows = [("glu", 4, [KFULL] * 2), ("short", 4, [KFULL] * 3), ("kv", 1, [KFULL] * 2),
            ("q", 2, [KFULL] * 2),
            ("B", 4, [KFULL, KHALF] * 2), ("C", 4, [KFULL, KHALF] * 2), ("A", 4, [KFULL, KHALF] * 2),
            ("mix", 4, [KFULL] * 2)]
    phases, s, g = {}, 0, 0
    for name, trips, groups in rows:
        ph = phases[name] = Phase(name, trips, groups, s, g)
        s, g = s + trips * ph.nslabs, g + trips * ph.ngroups
    for name in ("up", "down"):
        ph = phases[name] = Phase(name, 4, [KFULL] * 2, s, g)
        s, g = s + 4 * ph.nslabs, g + 4 * ph.ngroups
    return phases


PH = plan()
CHUNKS = FF // D
CHUNK_SLABS = 2 * 4 * PH["up"].nslabs
CHUNK_GROUPS = 2 * 4 * PH["up"].ngroups
TOTAL = PH["up"].slab0 + CHUNKS * CHUNK_SLABS

CONV_SHORT = dict(enumerate([3, 2, 2, 1, 2, 2, 2, 0, 2, 2, 2, 0]))
CONV_B = {k: int(k != 4) for k in range(12)}
assert sum(CONV_SHORT.values()) + sum(CONV_B.values()) == TAPS


def walk(eng, body):
    def loop(name, c=0, first=0):
        with eng.Fori(first, PH[name].trips) as t:
            body(PH[name], c, t)

    body(PH["glu"], 0, 0)
    loop("glu", first=1)
    loop("short")
    body(PH["kv"], 0, 0)
    for t in range(PH["q"].trips):
        body(PH["q"], 0, t)
    body("v tokens", 0, 0)
    loop("B")
    for t in range(PH["C"].trips):
        body(PH["C"], 0, t)
    loop("A")
    loop("mix")
    body(PH["up"], 0, 0)
    loop("up", first=1)
    loop("down")
    with eng.Fori(1, CHUNKS - 1) as c:
        loop("up", c)
        loop("down", c)
    loop("up", CHUNKS - 1)
    for t in range(PH["down"].trips):
        body(PH["down"], CHUNKS - 1, t)


def slab_of(ph, c, t, k):
    return ph.slab0 + k + t * ph.nslabs + c * CHUNK_SLABS


def group_of(ph, c, t, n):
    return ph.group0 + n + t * ph.ngroups + c * CHUNK_GROUPS


def build(nc, x, norm_mix_g, w_in, gate_b, conf_dw, conf_ln_g, conf_ln_b, w_conf_out, sconv_w,
          w_sconv_out, sinks, w_attn_out, w_mix_out, norm_ffn_g, w_up, w_down, final_g, out):
    w_in, w_conf_out, w_sconv_out = w_in[0], w_conf_out[0], w_sconv_out[0]
    w_attn_out, w_mix_out, w_up, w_down = w_attn_out[0], w_mix_out[0], w_up[0], w_down[0]

    ctx = ExitStack()
    with ctx:
        def sb(name, shape, dt=F32):
            return ctx.enter_context(nc.sbuf_tensor(name, shape, dt))

        def sem(name):
            return ctx.enter_context(nc.semaphore(name))

        w_raw = sb("w_raw", [P, RING, KT, COLS])
        w_hi = sb("w_hi", [P, RING, KT, COLS], F32R)
        w_lo = sb("w_lo", [P, RING, KT, COLS], F32R)
        res = sb("res", [P, NT, SEQ])
        h_hl = sb("h_hl", [P, NT, 2, SEQ], F32R)
        z_ba = sb("z_ba", [P, HT, 2, SEQ], F32R)
        merged = sb("merged", [P, NT, SEQ])
        PADL = TAPS - 1
        GLU_AT = HT * 2 * SEQ
        CONV_AT = GLU_AT + HT * (PADL + SEQ)
        REGION = CONV_AT + HT * SEQ
        region = sb("region", [P, REGION])

        def view(name, whole, offset, shape, dt=F32):
            return nc.alloc_sbuf_tensor_at(name, shape, dt, offset=nc.lookup_mloc(whole).addr + 4 * offset)

        z_c = view("z_c", region, 0, [P, HT, 2, SEQ], F32R)
        glu = view("glu", region, GLU_AT, [P, HT, PADL + SEQ])
        conv = view("conv", region, CONV_AT, [P, HT, SEQ])
        m_hl = view("m_hl", region, 0, [P, NT, 2, SEQ], F32R)
        x_tok = view("x_tok", region, 0, [P, 2, D])
        dw_rows = view("dw_rows", region, GLU_AT, [TAPS, W2])
        y_tok = view("y_tok", merged, 0, [P, 2, D])

        q_t = sb("q_t", [P, HT, SEQ])
        k_dup = sb("k_dup", [P, KVH, SEQ])
        v_tok = sb("v_tok", [P, 2, KVW])
        pair = [sb(f"pair{i}", [P, 2, SEQ]) for i in range(3)]
        gate = sb("gate", [P, 2, SEQ])
        gated = sb("gated", [P, 2, (TAPS3 - 1) + SEQ])
        probs = sb("probs", [P, 2, 2, SC])
        probs_t = sb("probs_t", [P, 2, SC])
        q_now = sb("q_now", [P, 2, SEQ])
        k_now = sb("k_now", [P, 1, SEQ])
        v_now = sb("v_now", [P, 2, P])
        mask = sb("mask", [P, SC])
        ident = sb("ident", [P, P])
        ones = sb("ones", [P, P])
        rstd = sb("rstd", [P, SEQ])
        stat = sb("stat", [P, SEQ])
        rows_g = sb("rows_g", [NT, P])
        rows_a = sb("rows_a", [PR_A, P])
        rows_b = sb("rows_b", [PR_B, P])
        par = sb("par", [P, 512])
        sinkb = sb("sinkb", [P, HEADS])
        top = sb("top", [P, 2, 2, 2])
        neg_top = sb("neg_top", [P, 2, 2, 2])
        sink_d = sb("sink_d", [P, 2, 2, 2])
        sink_e = sb("sink_e", [P, 2, 2, 2])
        denom = sb("denom", [P, 2, 2, 2])
        rdenom = sb("rdenom", [P, 2, 2, 2])
        tok_stat = sb("tok_stat", [P, 4, 2])

        acc = ctx.enter_context(nc.psum_tensor("acc", [P, 8, 512], F32))
        aux = [acc[:, 4 + i, :] for i in range(4)]

        raw_full = [sem(f"raw_full{i}") for i in range(RING)]
        hi_done, lo_done, slab_used, evac_done = sem("hi_done"), sem("lo_done"), sem("slab_used"), sem("evac_done")
        zeroed, consts, par_t, par_ok = sem("zeroed"), sem("consts"), sem("par_t"), sem("par_ok")
        warm, rows_g_in, rows_in = sem("warm"), sem("rows_g_in"), sem("rows_in")
        x_in = [sem(f"x_in{i}") for i in range(4)]
        x_t, x_copied, x_hi, x_hi2, h_lo, x_sq = (sem(n) for n in ("x_t", "x_copied", "x_hi", "x_hi2", "h_lo", "x_sq"))
        fold1, stat1, var1, root1, rstd1 = sem("fold1"), sem("stat1"), sem("var1"), sem("root1"), sem("rstd1")
        glu_sig, glu_done, gated_done, short_step, z_b_f, z_b_hi, z_b_lo = (sem(n) for n in (
            "glu_sig", "glu_done", "gated_done", "short_step", "z_b_f", "z_b_hi", "z_b_lo"))
        conv_a, conv_b, conv_c = sem("conv_a"), sem("conv_b"), sem("conv_c")
        k_in, v_t, v_copied = sem("k_in"), sem("v_t"), sem("v_copied")
        q_ready, v_ready, s_ready, masked, top_step, exp_done, norm_step, t_ready, t_copied, o_ready, o_step = (
            sem(n) for n in ("q_ready", "v_ready", "s_ready", "masked", "top_step", "exp_done", "norm_step",
                             "t_ready", "t_copied", "o_ready", "o_step"))
        ln_v, ln_pe, ln_act = sem("ln_v"), sem("ln_pe"), sem("ln_act")
        gate_sig, m_sum, m_hi, m_lo = sem("gate_sig"), sem("m_sum"), sem("m_hi"), sem("m_lo")
        r_hi, r_sq, r_lo, r_sum = sem("r_hi"), sem("r_sq"), sem("r_lo"), sem("r_sum")
        fold2, stat2, var2, root2, rstd2 = sem("fold2"), sem("stat2"), sem("var2"), sem("root2"), sem("rstd2")
        hid_f, hid_hi, hid_lo = sem("hid_f"), sem("hid_hi"), sem("hid_lo")
        y_g, y_sq, y_t, y_copied, y_sum = sem("y_g"), sem("y_sq"), sem("y_t"), sem("y_copied"), sem("y_sum")
        fold3, stat3, var3, root3, rstd3, stored = (sem(n) for n in (
            "fold3", "stat3", "var3", "root3", "rstd3", "stored"))

        scaled = [sem("scaled0"), sem("scaled1")]

        block = ctx.enter_context(nc.Block())

        def both(t2):
            return t2[:, None, :].to_broadcast((P, 2, SEQ))

        def bank(ph, n):
            return 2 * n if ph.ngroups == 3 else 2 * (n % 2)

        @block.sync
        def _(sp):
            def load_x(i):
                cols = slice(i * D // 4, (i + 1) * D // 4)
                sp.dma_start(x_tok[:, :, cols], x[0][:, cols].rearrange("(b p) n -> p b n", p=P)).then_inc(x_in[i], 16)

            def load_slab(ph, c, t, k):
                n, i, _ = ph.slabs[k]
                s = slab_of(ph, c, t, k)
                if ph.name in ("B", "C", "A"):
                    b = {"A": 0, "B": 1, "C": 2}[ph.name]
                    col = t * (2 * COLS) + (n // 2) * COLS
                    if n % 2:
                        w = (w_conf_out, w_sconv_out, w_attn_out)[b]
                    else:
                        w, col = w_in, col + (C_G + b * D)
                    row = i * ROWS
                else:
                    w, starts = {"glu": (w_in, (C_AVAL, C_AGATE)), "short": (w_in, (C_C, C_BH, C_B)),
                                 "kv": (w_in, (C_K, C_V)), "q": (w_in, (C_Q, C_Q + COLS)),
                                 "mix": (w_mix_out, (0, COLS)), "up": (w_up, (0, COLS)),
                                 "down": (w_down, (0, COLS))}[ph.name]
                    step = COLS * (1 if ph.name in ("glu", "short") else 2)
                    col = t * step + starts[n]
                    row = i * ROWS
                    if ph.name == "up":
                        col = c * D + col
                    if ph.name == "down":
                        row = c * D + row
                shared = ph.name in ("B", "A")
                if not (isinstance(s, int) and s < RING or shared and k == 4):
                    sp.wait_ge(lo_done, s + (shared and k == 3) - (RING - 1))
                sp.dma_start(w_raw[:, k % RING], w[bass.ds(row, ROWS), bass.ds(col, COLS)]
                             .rearrange("(a p) n -> p a n", p=P)).then_inc(raw_full[k % RING], 16)

            def trip(ph, c, t):
                if ph == "v tokens":
                    return
                for k in range(ph.nslabs):
                    if ph.name == "glu" and isinstance(t, int) and t == 0 and k == 1:
                        load_x(2)
                        load_x(3)
                    if ph.name == "glu" and isinstance(t, int) and t == 0 and k == 3:
                        load_rows()
                    if ph.name == "q" and k == 2 and t == 0:
                        sp.wait_ge(evac_done, PH["kv"].group0 + 1)
                        for half in range(2):
                            for odd in range(2):
                                sp.dma_start(k_dup[half * HD:(half + 1) * HD, odd:KVH:2, :],
                                             pair[0][odd * HD:(odd + 1) * HD, :, :]).then_inc(k_in, 16)
                    load_slab(ph, c, t, k)

            def rows(dst, src, done):
                sp.dma_start(dst, src).then_inc(done, 16)

            def load_rows():
                rows(rows_a[0:48, :], gate_b[0].rearrange("b (t p) -> (b t) p", p=P), rows_in)
                rows(rows_a[48:64, :], norm_ffn_g[0].rearrange("(t p) -> t p", p=P), rows_in)
                rows(rows_a[64:80, :], final_g.rearrange("(t p) -> t p", p=P), rows_in)
                rows(rows_b[0:8, :], conf_ln_g[0].rearrange("(t p) -> t p", p=P), rows_in)
                rows(rows_b[8:16, :], conf_ln_b[0].rearrange("(t p) -> t p", p=P), rows_in)
                rows(rows_b[16:40, :], sconv_w[0].rearrange("k (t p) -> (k t) p", p=P), rows_in)
                rows(dw_rows[:, :], conf_dw[0], rows_in)
                rows(sinkb[:, :], sinks.to_broadcast((P, HEADS)), rows_in)

            rows(rows_g[:, :], norm_mix_g[0].rearrange("(t p) -> t p", p=P), rows_g_in)
            load_x(0)
            load_x(1)
            walk(sp, trip)
            for i in range(4):
                b, cols = i % 2, slice((i // 2) * W2, (i // 2 + 1) * W2)
                sp.wait_ge(scaled[b], i // 2 + 1)
                sp.dma_start(out[0][b * P:(b + 1) * P, cols], y_tok[:, b, cols]).then_inc(stored, 16)
            sp.wait_ge(stored, 64)

        @block.gpsimd
        def _(pool):
            pool.memset(ident[:, :], 0.0).then_inc(zeroed, 1)
            pool.memset(ones[:, :], 1.0).then_inc(consts, 1)
            pool.wait_ge(zeroed, 1)
            pool.affine_select(out=ident[:, :], in_=ident[:, :], compare_op=ALU.not_equal, fill=1.0, base=0,
                               pattern=[[-1, P]], channel_multiplier=1).then_inc(consts, 1)
            pool.memset(mask[:, :], 0.0).then_inc(zeroed, 1)
            pool.wait_ge(zeroed, 2)
            for lo in (0, 2 * BLK):
                pool.affine_select(out=mask[:, lo:lo + BLK], in_=mask[:, lo:lo + BLK], compare_op=ALU.is_ge,
                                   fill=MASKED, base=0, pattern=[[-1, BLK]], channel_multiplier=1).then_inc(consts, 1)
            pool.affine_select(out=mask[:, BLK:2 * BLK], in_=mask[:, BLK:2 * BLK], compare_op=ALU.is_ge,
                               fill=MASKED, base=-1, pattern=[[1, BLK]], channel_multiplier=-1).then_inc(consts, 1)
            for i in range(8):
                pool.wait_ge(x_copied, i + 1)
                tiles = slice(2 * i, 2 * i + 2)
                pool.tensor_tensor(merged[:, tiles, :], res[:, tiles, :], res[:, tiles, :], ALU.mult).then_inc(x_sq, 1)
            pool.wait_ge(x_sq, 8)
            for n, w in enumerate((8, 4, 2, 1)):
                if n:
                    pool.wait_ge(fold1, n)
                pool.tensor_tensor(merged[:, 0:w, :], merged[:, 0:w, :], merged[:, w:2 * w, :], ALU.add).then_inc(fold1, 1)

        @block.scalar
        def _(act):
            def hi(ph, c, t, k):
                s = slab_of(ph, c, t, k)
                if isinstance(s, int) and s + LOOKAHEAD >= TOTAL:
                    return
                ahead = k + LOOKAHEAD
                act.wait_ge(raw_full[ahead % RING], 16 * (ph.slab0 // RING + ahead // RING + 1)
                            + t * (16 * ph.nslabs // RING) + c * (16 * CHUNK_SLABS // RING))
                if not (isinstance(s, int) and s == 0):
                    act.wait_ge(slab_used, s)
                act.activation(w_hi[:, ahead % RING], w_raw[:, ahead % RING], ACT.Copy).then_inc(hi_done, 1)

            def start_pair(i):
                act.wait_ge(x_t, i + 1)
                act.activation(res[:, 2 * i:2 * i + 2, :], aux[i % 3][:, :].rearrange("p (e n) -> p e n", e=2),
                               ACT.Copy).then_inc(x_copied, 1)
                act.wait_ge(x_copied, i + 1)
                act.activation(h_hl[:, 2 * i, 0, :], res[:, 2 * i, :], ACT.Copy,
                               scale=par[:, PR_G1 + 2 * i:PR_G1 + 2 * i + 1]).then_inc(x_hi, 1)

            def prologue(s):
                act.wait_ge(raw_full[s], 16)
                act.activation(w_hi[:, s], w_raw[:, s], ACT.Copy).then_inc(hi_done, 1)

            act.wait_ge(consts, 1)
            act.activation(tok_stat[:, 1, 0:1], ones[:, 0:1], ACT.Sqrt).then_inc(warm, 1)
            act.wait_ge(par_ok, 1)
            for i in range(8):
                start_pair(i)
                if i in (3, 5, 7):
                    prologue((i - 3) // 2)

            def gates(ph, t, n, b):
                g = group_of(ph, 0, t, n)
                act.wait_ge(evac_done, g + 1)
                for e in range(2):
                    col = t * 4 + (PR_GB + b * NT + n + e)
                    act.activation(gate[:, e, :], pair[0][:, e, :], ACT.Sigmoid,
                                   bias=par[:, bass.ds(col, 1)]).then_inc(gate_sig, 1)

            def exps(t, p, e):
                act.wait_ge(top_step, t * 10 + 5 * p + 5)
                for b, cols in ((0, slice(0, BLK)), (1, slice(BLK, SC))):
                    act.activation(probs[:, p, e, cols], probs[:, p, e, cols], ACT.Exp,
                                   bias=neg_top[:, p, e, b:b + 1],
                                   accum_out=denom[:, p, e, b:b + 1]).then_inc(exp_done, 1)
                if e == 1:
                    act.activation(sink_e[:, p], sink_d[:, p], ACT.Exp).then_inc(exp_done, 1)

            def copy_t(t, p):
                act.wait_ge(t_ready, t * 2 + p + 1)
                if p == 1:
                    act.wait_ge(o_ready, t * 2 + 1)
                for e in range(2):
                    act.activation(probs_t[:, e, :], aux[2 + e][:, 0:SC], ACT.Copy).then_inc(t_copied, 1)

            def ln_square(i):
                act.wait_ge(ln_v, 6 + i)
                act.activation(glu[:, 4 * i:4 * i + 4, 0:SEQ], conv[:, 4 * i:4 * i + 4, :], ACT.Square).then_inc(ln_act, 1)

            def ln_root():
                act.wait_ge(ln_v, 12)
                act.activation(stat[:, :], stat[:, :], ACT.Sqrt).then_inc(ln_act, 1)

            def ln_sigmoid(i):
                act.wait_ge(ln_v, 19 + 4 * i)
                act.activation(glu[:, 4 * i:4 * i + 4, 0:SEQ], conv[:, 4 * i:4 * i + 4, :],
                               ACT.Sigmoid).then_inc(ln_act, 1)

            def ln_hi(i):
                act.wait_ge(ln_v, 24 + i)
                act.activation(z_ba[:, 4 * i:4 * i + 4, 0, :], conv[:, 4 * i:4 * i + 4, :], ACT.Copy).then_inc(ln_act, 1)

            LN = {23: lambda: ln_square(0), 24: lambda: ln_square(1), 28: ln_root, 34: lambda: ln_sigmoid(0),
                  35: lambda: ln_sigmoid(1), 38: lambda: ln_hi(0), 40: lambda: ln_hi(1)}

            def trip(ph, c, t):
                if ph == "v tokens":
                    return
                for k in range(ph.nslabs):
                    hi(ph, c, t, k)
                    n, i, size = ph.slabs[k]
                    ends = i == size - 1
                    g = group_of(ph, c, t, n)
                    if ph.name == "glu":
                        if isinstance(t, int) and t == 0 and k == 3:
                            act.wait_ge(var1, 1)
                            act.activation(rstd[:, :], stat[:, :], ACT.Sqrt).then_inc(root1, 1)
                        if ends and n == 1:
                            act.wait_ge(evac_done, g + 1)
                            act.activation(gate[:, :, :], pair[1][:, :, :], ACT.Sigmoid).then_inc(glu_sig, 1)
                    if ph.name == "short" and ends and n == 2:
                        act.wait_ge(z_b_f, t + 1)
                        act.activation(z_ba[:, bass.ds(t * 2, 2), 0, :], pair[2][:, :, :], ACT.Copy).then_inc(z_b_hi, 1)
                    if ph.name == "B":
                        if k == 0:
                            act.wait_ge(evac_done, PH["q"].group0 + 4)
                            act.activation(q_now[:, :, :], q_t[:, bass.ds(t * 2, 2), :], ACT.Copy,
                                           scale=float(HD) ** -0.5).then_inc(q_ready, 1)
                            act.wait_ge(k_in, 64)
                            act.activation(k_now[:, :, :], k_dup[:, bass.ds(t, 1), :], ACT.Copy).then_inc(q_ready, 1)
                        if k == 3:
                            exps(t, 0, 0)
                            exps(t, 0, 1)
                        if k in (5, 6):
                            exps(t, 1, k - 5)
                        if k in (7, 9):
                            copy_t(t, k // 9)
                    if ph.name in ("B", "C", "A") and ends and n % 2 == 0:
                        gates(ph, t, n, {"A": 0, "B": 1, "C": 2}[ph.name])
                    if ph.name == "C" and t * ph.nslabs + k in LN:
                        LN[t * ph.nslabs + k]()
                    if ph.name == "A" and ends and n % 2 == 1:
                        j = t * 2 + n // 2
                        act.wait_ge(m_sum, j + 9)
                        act.activation(m_hl[:, bass.ds(j * 2, 2), 0, :], merged[:, bass.ds(j * 2, 2), :],
                                       ACT.Copy).then_inc(m_hi, 1)
                    if ph.name == "mix" and ends:
                        j = t * 2 + n
                        act.wait_ge(evac_done, g + 1)
                        for e in range(2):
                            act.activation(h_hl[:, bass.ds(j * 2 + e, 1), 0, :], res[:, bass.ds(j * 2 + e, 1), :], ACT.Copy,
                                           scale=par[:, bass.ds(j * 2 + (PR_G2 + e), 1)]).then_inc(r_hi, 1)
                        act.activation(pair[n][:, :, :], res[:, bass.ds(j * 2, 2), :], ACT.Square).then_inc(r_sq, 1)
                    if ph.name == "up":
                        if isinstance(t, int) and t == 0 and k == 2:
                            act.wait_ge(var2, 1)
                            act.activation(rstd[:, :], stat[:, :], ACT.Sqrt).then_inc(root2, 1)
                        if ends:
                            j = t * 2 + n
                            act.wait_ge(hid_f, c * 8 + j + 1)
                            act.activation(m_hl[:, bass.ds(j * 2, 2), 0, :], pair[n][:, :, :], ACT.Copy).then_inc(hid_hi, 1)
                    if ph.name == "down" and isinstance(c, int) and c == CHUNKS - 1 and ends:
                        j = 2 * t + n
                        act.wait_ge(evac_done, g + 1)
                        if j >= 2:
                            act.wait_ge(y_t, j - 1)
                        for e in range(2):
                            act.activation(pair[n][:, e, :], res[:, 2 * j + e, :], ACT.Copy,
                                           scale=par[:, PR_GF + 2 * j + e:PR_GF + 2 * j + e + 1]).then_inc(y_g, 1)
                        if j >= 2:
                            act.wait_ge(y_sum, j - 1)
                        act.activation((pair[2], gate)[n][:, :, :], res[:, 2 * j:2 * j + 2, :], ACT.Square).then_inc(y_sq, 1)

            walk(act, trip)
            act.wait_ge(var3, 1)
            act.activation(tok_stat[:, 1, :], tok_stat[:, 0, :], ACT.Sqrt).then_inc(root3, 1)
            act.wait_ge(rstd3, 1)
            act.wait_ge(y_copied, 8)
            for i in range(2):
                act.activation(y_tok[:, 1, i * W2:(i + 1) * W2], y_tok[:, 1, i * W2:(i + 1) * W2], ACT.Copy,
                               scale=tok_stat[:, 2, 1:2]).then_inc(scaled[1], 1)

        @block.vector
        def _(dve):
            def lo(ph, c, t, k):
                s = slab_of(ph, c, t, k)
                if isinstance(s, int) and s + LOOKAHEAD >= TOTAL:
                    return
                q = (k + LOOKAHEAD) % RING
                dve.wait_ge(hi_done, s + (LOOKAHEAD + 1))
                dve.tensor_tensor(w_lo[:, q], w_raw[:, q], w_hi[:, q].bitcast(F32), ALU.subtract).then_inc(lo_done, 1)

            def prologue(s):
                dve.wait_ge(hi_done, s + 1)
                dve.tensor_tensor(w_lo[:, s], w_raw[:, s], w_hi[:, s].bitcast(F32), ALU.subtract).then_inc(lo_done, 1)

            def start_pair(i):
                tiles = (2 * i + 1, 2 * i)
                gain = [par[:, PR_G1 + tile:PR_G1 + tile + 1] for tile in tiles]
                dve.wait_ge(x_copied, i + 1)
                dve.tensor_scalar(h_hl[:, tiles[0], 0, :], res[:, tiles[0], :], gain[0], None, ALU.mult).then_inc(x_hi2, 1)
                dve.wait_ge(x_hi, i + 1)
                dve.wait_ge(x_hi2, i + 1)
                for tile, g in zip(tiles, gain):
                    dve.scalar_tensor_tensor(h_hl[:, tile, 1, :], res[:, tile, :], g, h_hl[:, tile, 0, :].bitcast(F32),
                                             ALU.mult, ALU.subtract).then_inc(h_lo, 1)

            dve.wait_ge(par_t, 1)
            dve.tensor_copy(par[:, PR_G1:PR_G1 + NT], aux[3][:, PR_G1:PR_G1 + NT]).then_inc(par_ok, 1)
            dve.wait_ge(par_ok, 1)
            for i in range(8):
                start_pair(i)
                if i in (3, 5, 7):
                    prologue((i - 3) // 2)

            def parameters():
                dve.memset(gated[:, :, 0:TAPS3 - 1], 0.0).then_inc(par_ok, 1)
                dve.wait_ge(par_t, 2)
                dve.tensor_copy(par[:, 0:PR_A], aux[3][:, 0:PR_A]).then_inc(par_ok, 1)
                dve.tensor_copy(par[:, PR_LNG:PR_LNG + PR_B], aux[3][:, PR_LNG:PR_LNG + PR_B]).then_inc(par_ok, 1)
                dve.tensor_copy(par[:, PR_DW:PR_DW + HT * TAPS], aux[3][:, PR_DW:PR_DW + HT * TAPS]).then_inc(par_ok, 1)
                dve.memset(glu[:, :, 0:PADL], 0.0).then_inc(par_ok, 1)

            def mean_eps(dst, src, scale, eps, done):
                dve.tensor_scalar(dst, src, scale, eps, ALU.mult, ALU.add).then_inc(done, 1)

            def tap(tile, k, step, at):
                w = par[:, bass.ds(tile * TAPS + (PR_DW + k), 1)]
                src = glu[:, bass.ds(tile, 1), k:k + SEQ]
                dst = conv[:, bass.ds(tile, 1), :]
                if k == 0:
                    dve.tensor_scalar(dst, src, w, None, ALU.mult).then_inc(step, 1)
                else:
                    if at is not None:
                        dve.wait_ge(step, at)
                    dve.scalar_tensor_tensor(dst, src, w, dst, ALU.mult, ALU.add).then_inc(step, 1)

            def top_of(t, p):
                dve.wait_ge(s_ready, t * 2 + p + 1)
                for e in range(2):
                    dve.tensor_tensor(probs[:, p, e, :], aux[e][:, 0:SC], mask[:, :], ALU.add).then_inc(masked, 1)
                dve.wait_ge(masked, t * 4 + 2 * p + 2)
                dve.reduce_max(top[:, p, :, 0], probs[:, p, :, 0:BLK], AX.X).then_inc(top_step, 1)
                dve.reduce_max(top[:, p, :, 1], probs[:, p, :, BLK:SC], AX.X).then_inc(top_step, 1)
                dve.wait_ge(top_step, t * 10 + 5 * p + 2)
                sink = sinkb[:, bass.ds(t * 4 + 2 * p, 2)][:, :, None].to_broadcast((P, 2, 2))
                dve.tensor_tensor(top[:, p], top[:, p], sink, ALU.max).then_inc(top_step, 1)
                dve.wait_ge(top_step, t * 10 + 5 * p + 3)
                dve.tensor_scalar(neg_top[:, p], top[:, p], -1.0, None, ALU.mult).then_inc(top_step, 1)
                dve.tensor_tensor(sink_d[:, p], sink, top[:, p], ALU.subtract).then_inc(top_step, 1)

            def normalise(t, p):
                dve.wait_ge(exp_done, t * 10 + 5 * p + 5)
                dve.tensor_tensor(denom[:, p], denom[:, p], sink_e[:, p], ALU.add).then_inc(norm_step, 1)
                dve.wait_ge(norm_step, t * 12 + 6 * p + 1)
                dve.reciprocal(rdenom[:, p], denom[:, p]).then_inc(norm_step, 1)
                dve.wait_ge(norm_step, t * 12 + 6 * p + 2)
                for e in range(2):
                    for b, cols in ((0, slice(0, BLK)), (1, slice(BLK, SC))):
                        dve.tensor_scalar(probs[:, p, e, cols], probs[:, p, e, cols], rdenom[:, p, e, b:b + 1], None,
                                          ALU.mult).then_inc(norm_step, 1)

            def head_out(t, p):
                dve.wait_ge(o_ready, t * 2 + p + 1)
                j = t * 2 + p
                for e in range(2):
                    part = slice(e * HD, (e + 1) * HD)
                    dve.tensor_copy(z_c[part, bass.ds(j, 1), 0, :], aux[p][part, None, e * SEQ:(e + 1) * SEQ]).then_inc(o_step, 1)
                dve.wait_ge(o_step, t * 8 + 4 * p + 2)
                for e in range(2):
                    part = slice(e * HD, (e + 1) * HD)
                    dve.tensor_tensor(z_c[part, bass.ds(j, 1), 1, :], aux[p][part, None, e * SEQ:(e + 1) * SEQ],
                                      z_c[part, bass.ds(j, 1), 0, :].bitcast(F32), ALU.subtract).then_inc(o_step, 1)

            def ln_fold(src, base):
                for n, (dst, a, b) in enumerate((
                        (pair[2][:, :, :], src(0, 2), src(2, 4)), (pair[1][:, :, :], src(4, 6), src(6, 8)),
                        (pair[2][:, :, :], pair[2][:, :, :], pair[1][:, :, :]),
                        (stat[:, :], pair[2][:, 0, :], pair[2][:, 1, :]))):
                    if n >= 2:
                        dve.wait_ge(ln_v, base + n)
                    dve.tensor_tensor(dst, a, b, ALU.add).then_inc(ln_v, 1)

            def ln_sum():
                dve.wait_ge(conv_b, 4 * 11)
                dve.wait_ge(conv_c, 4 * TAPS)
                dve.wait_ge(m_sum, 3)
                ln_fold(lambda a, b: conv[:, a:b, :], 0)

            def ln_center():
                dve.wait_ge(ln_pe, 1)
                mean_eps(stat[:, :], aux[2][:, 0:SEQ], 1.0 / W2, 0.0, ln_v)
                dve.wait_ge(ln_v, 5)
                for i in range(2):
                    dve.tensor_tensor(conv[:, 4 * i:4 * i + 4, :], conv[:, 4 * i:4 * i + 4, :],
                                      stat[:, None, :].to_broadcast((P, 4, SEQ)), ALU.subtract).then_inc(ln_v, 1)

            def ln_sum2():
                dve.wait_ge(ln_act, 2)
                dve.wait_ge(m_sum, 4)
                ln_fold(lambda a, b: glu[:, a:b, 0:SEQ], 7)

            def ln_var():
                dve.wait_ge(ln_pe, 2)
                mean_eps(stat[:, :], aux[2][:, 0:SEQ], 1.0 / W2, LN_EPS, ln_v)

            def ln_rstd():
                dve.wait_ge(ln_act, 3)
                dve.reciprocal(stat[:, :], stat[:, :]).then_inc(ln_v, 1)
                dve.wait_ge(ln_v, 13)
                for i in range(2):
                    dve.tensor_tensor(conv[:, 4 * i:4 * i + 4, :], conv[:, 4 * i:4 * i + 4, :],
                                      stat[:, None, :].to_broadcast((P, 4, SEQ)), ALU.mult).then_inc(ln_v, 1)

            def ln_affine():
                dve.wait_ge(ln_v, 15)
                for j in range(HT):
                    dve.tensor_scalar(conv[:, j, :], conv[:, j, :], par[:, PR_LNG + j:PR_LNG + j + 1],
                                      par[:, PR_LNB + j:PR_LNB + j + 1], ALU.mult, ALU.add).then_inc(ln_v, 1)

            def ln_silu(i):
                dve.wait_ge(ln_act, 4 + i)
                dve.tensor_tensor(conv[:, 4 * i:4 * i + 4, :], conv[:, 4 * i:4 * i + 4, :],
                                  glu[:, 4 * i:4 * i + 4, 0:SEQ], ALU.mult).then_inc(ln_v, 1)

            def ln_lo(i):
                dve.wait_ge(ln_act, 6 + i)
                dve.tensor_tensor(z_ba[:, 4 * i:4 * i + 4, 1, :], conv[:, 4 * i:4 * i + 4, :],
                                  z_ba[:, 4 * i:4 * i + 4, 0, :].bitcast(F32), ALU.subtract).then_inc(ln_v, 1)

            LN = {20: ln_sum, 22: ln_center, 26: ln_sum2, 28: ln_var, 30: ln_rstd, 32: ln_affine, 36: lambda: ln_silu(0),
                  37: lambda: ln_silu(1), 40: lambda: ln_lo(0), 42: lambda: ln_lo(1)}

            taps_c = [(tile0 + e, k) for tile0 in (4, 6) for k in range(TAPS) for e in range(2)]
            done_c = [0]

            def taps_static(n):
                for tile, k in taps_c[done_c[0]:done_c[0] + n]:
                    tap(tile, k, conv_c, done_c[0] - 1)
                    done_c[0] += 1

            def trip(ph, c, t):
                if ph == "v tokens":
                    dve.wait_ge(v_t, 1)
                    dve.tensor_copy(v_tok[:, :, :].rearrange("p b n -> p (b n)"), aux[2][:, :]).then_inc(v_copied, 1)
                    return
                for k in range(ph.nslabs):
                    if ph.name == "B" and k in (4, 7):
                        normalise(t, k // 7)
                    lo(ph, c, t, k)
                    n, i, size = ph.slabs[k]
                    s, g, ends = slab_of(ph, c, t, k), group_of(ph, c, t, n), i == size - 1
                    if ph.name == "glu" and isinstance(t, int) and t == 0:
                        if k == 3:
                            dve.wait_ge(stat1, 1)
                            mean_eps(stat[:, :], aux[2][:, 0:SEQ], 1.0 / D, RMS_EPS, var1)
                            dve.wait_ge(root1, 1)
                            dve.reciprocal(rstd[:, :], rstd[:, :]).then_inc(rstd1, 1)
                            dve.wait_ge(rstd1, 1)
                        if k == 4:
                            parameters()
                    if ph.name == "up" and isinstance(t, int) and t == 0:
                        if k == 0:
                            dve.wait_ge(r_sum, 9)
                            dve.tensor_tensor(stat[:, :], pair[2][:, 0, :], pair[2][:, 1, :], ALU.add).then_inc(fold2, 1)
                        if k == 1:
                            dve.wait_ge(stat2, 1)
                            mean_eps(stat[:, :], aux[2][:, 0:SEQ], 1.0 / D, RMS_EPS, var2)
                        if k == 2:
                            dve.wait_ge(root2, 1)
                            dve.reciprocal(rstd[:, :], rstd[:, :]).then_inc(rstd2, 1)
                            dve.wait_ge(rstd2, 1)
                    if ph.name == "short":
                        if k == 0:
                            dve.wait_ge(glu_done, 4)
                            dve.wait_ge(par_ok, 6)
                        first = sum(CONV_SHORT[m] for m in range(k))
                        for m in range(first, first + CONV_SHORT[k]):
                            tap(t, m, conv_a, t * 20 + m)
                        if k in (8, 9, 10):
                            m = k - 8
                            for e in range(2):
                                src = gated[:, e, m:m + SEQ]
                                w = par[:, bass.ds(t * 2 + (PR_W3 + m * HT + e), 1)]
                                if m == 0:
                                    dve.wait_ge(gated_done, t + 1)
                                    dve.tensor_scalar(pair[1][:, e, :], src, w, None, ALU.mult).then_inc(short_step, 1)
                                else:
                                    dve.wait_ge(short_step, t * 6 + (2 * (m - 1) + e + 1))
                                    dve.scalar_tensor_tensor(pair[1][:, e, :], src, w, pair[1][:, e, :], ALU.mult,
                                                             ALU.add).then_inc(short_step, 1)
                    if ph.name == "kv":
                        taps_static(3 if not ends else 2)
                    if ph.name == "q":
                        taps_static(4 if not ends else 2)
                    if ph.name == "B":
                        if k == 0:
                            dve.wait_ge(v_copied, 1)
                            dve.wait_ge(consts, 5)
                            for half in range(2):
                                dve.tensor_copy(v_now[:, :, half * HD:(half + 1) * HD],
                                                v_tok[:, :, bass.ds(t * HD, HD)]).then_inc(v_ready, 1)
                        if CONV_B[k]:
                            first = 20 + sum(CONV_B[m] for m in CONV_B if m < k)
                            for m in range(first, first + CONV_B[k]):
                                if m == 20:
                                    dve.wait_ge(conv_a, 80)
                                tap(t, m, conv_b, None if m == 20 else t * 11 + (m - 20))
                        if k in (2, 4):
                            top_of(t, k // 4)
                        if k == 9:
                            head_out(t, 0)
                    if ph.name == "C":
                        at = t * ph.nslabs + k
                        if at < 20:
                            taps_static(3 if not ends else 2)
                        if at in LN:
                            LN[at]()
                    if not ends:
                        continue
                    dve.wait_ge(slab_used, s + 1)
                    a = acc[:, bank(ph, n):bank(ph, n) + 2, 0:SEQ]
                    if ph.name in ("glu", "kv"):
                        dve.tensor_tensor(pair[n][:, :, :], a, both(rstd), ALU.mult).then_inc(evac_done, 1)
                        if ph.name == "glu" and n == 1:
                            dve.wait_ge(glu_sig, t + 1)
                            dve.tensor_tensor(glu[:, bass.ds(t * 2, 2), PADL:PADL + SEQ], pair[0][:, :, :],
                                              gate[:, :, :], ALU.mult).then_inc(glu_done, 1)
                    elif ph.name == "short":
                        dve.tensor_tensor(pair[n][:, :, :], a, both(rstd), ALU.mult).then_inc(evac_done, 1)
                        dve.wait_ge(evac_done, g + 1)
                        if n == 1:
                            dve.tensor_tensor(gated[:, :, TAPS3 - 1:], pair[0][:, :, :], pair[1][:, :, :],
                                              ALU.mult).then_inc(gated_done, 1)
                        if n == 2:
                            dve.wait_ge(short_step, t * 6 + 6)
                            dve.tensor_tensor(pair[2][:, :, :], pair[2][:, :, :], pair[1][:, :, :], ALU.mult).then_inc(z_b_f, 1)
                            dve.wait_ge(z_b_hi, t + 1)
                            dve.tensor_tensor(z_ba[:, bass.ds(t * 2, 2), 1, :], pair[2][:, :, :],
                                              z_ba[:, bass.ds(t * 2, 2), 0, :].bitcast(F32), ALU.subtract).then_inc(z_b_lo, 1)
                    elif ph.name == "q":
                        j = t * 2 + n
                        dve.tensor_tensor(q_t[:, 2 * j:2 * j + 2, :], a, both(rstd), ALU.mult).then_inc(evac_done, 1)
                    elif ph.name in ("B", "C", "A") and n % 2 == 0:
                        dve.tensor_tensor(pair[0][:, :, :], a, both(rstd), ALU.mult).then_inc(evac_done, 1)
                    elif ph.name in ("B", "C", "A"):
                        j = t * 2 + n // 2
                        first = {"B": 0, "C": 16, "A": 32}[ph.name]
                        dve.wait_ge(gate_sig, j * 2 + (first + 2))
                        m = merged[:, bass.ds(j * 2, 2), :]
                        if ph.name == "B":
                            dve.tensor_tensor(m, a, gate[:, :, :], ALU.mult).then_inc(evac_done, 1)
                            if n == 3:
                                head_out(t, 1)
                        else:
                            dve.tensor_tensor(pair[1][:, :, :], a, gate[:, :, :], ALU.mult).then_inc(evac_done, 1)
                            dve.wait_ge(evac_done, g + 1)
                            dve.tensor_tensor(m, m, pair[1][:, :, :], ALU.add).then_inc(m_sum, 1)
                        if ph.name == "A":
                            dve.wait_ge(m_hi, j + 1)
                            dve.tensor_tensor(m_hl[:, bass.ds(j * 2, 2), 1, :], m,
                                              m_hl[:, bass.ds(j * 2, 2), 0, :].bitcast(F32), ALU.subtract).then_inc(m_lo, 1)
                    elif ph.name == "mix":
                        j = t * 2 + n
                        r = res[:, bass.ds(j * 2, 2), :]
                        dve.tensor_tensor(r, a, r, ALU.add).then_inc(evac_done, 1)
                        for e in range(2):
                            dve.wait_ge(r_hi, j * 2 + (e + 1))
                            dve.scalar_tensor_tensor(h_hl[:, bass.ds(j * 2 + e, 1), 1, :], res[:, bass.ds(j * 2 + e, 1), :],
                                                     par[:, bass.ds(j * 2 + (PR_G2 + e), 1)],
                                                     h_hl[:, bass.ds(j * 2 + e, 1), 0, :].bitcast(F32),
                                                     ALU.mult, ALU.subtract).then_inc(r_lo, 1)
                        dve.wait_ge(r_sq, j + 1)
                        dve.wait_ge(r_sum, j + 1)
                        dve.tensor_tensor(pair[2][:, :, :], pair[2][:, :, :], pair[n][:, :, :], ALU.add).then_inc(r_sum, 1)
                    elif ph.name == "up":
                        j = t * 2 + n
                        dve.tensor_tensor(pair[n][:, :, :], a, both(rstd), ALU.mult).then_inc(evac_done, 1)
                        dve.wait_ge(evac_done, g + 1)
                        dve.scalar_tensor_tensor(pair[n][:, :, :], pair[n][:, :, :], 0.0, pair[n][:, :, :], ALU.max,
                                                 ALU.mult).then_inc(hid_f, 1)
                        dve.wait_ge(hid_hi, c * 8 + j + 1)
                        dve.tensor_tensor(m_hl[:, bass.ds(j * 2, 2), 1, :], pair[n][:, :, :],
                                          m_hl[:, bass.ds(j * 2, 2), 0, :].bitcast(F32), ALU.subtract).then_inc(hid_lo, 1)
                    else:
                        j = t * 2 + n
                        r = res[:, bass.ds(j * 2, 2), :]
                        dve.tensor_tensor(r, a, r, ALU.add).then_inc(evac_done, 1)
                        if isinstance(c, int) and c == CHUNKS - 1:
                            finish_pair(j)
                if ph.name == "C" and t == PH["C"].trips - 1:
                    dve.memset(pair[2][:, :, :], 0.0).then_inc(r_sum, 1)

            def finish_pair(j):
                n = j % 2
                dve.wait_ge(y_sq, j + 1)
                src = (pair[2], gate)[n]
                if j == 0:
                    dve.tensor_copy(q_now[:, :, :], src[:, :, :]).then_inc(y_sum, 1)
                else:
                    dve.wait_ge(y_sum, j)
                    dve.tensor_tensor(q_now[:, :, :], q_now[:, :, :], src[:, :, :], ALU.add).then_inc(y_sum, 1)
                if j:
                    copy_y(j - 1)

            def copy_y(j):
                dve.wait_ge(y_t, j + 1)
                dve.tensor_copy(y_tok[:, :, 2 * j * P:(2 * j + 2) * P],
                                aux[j % 2][:, :].rearrange("p (b n) -> p b n", b=2)).then_inc(y_copied, 1)

            walk(dve, trip)
            dve.wait_ge(y_sum, 8)
            dve.tensor_tensor(stat[:, :], q_now[:, 0, :], q_now[:, 1, :], ALU.add).then_inc(fold3, 1)
            copy_y(7)
            dve.wait_ge(stat3, 1)
            mean_eps(tok_stat[:, 0, :], aux[2][:, 0:2], 1.0 / D, RMS_EPS, var3)
            dve.wait_ge(root3, 1)
            dve.reciprocal(tok_stat[:, 2, :], tok_stat[:, 1, :]).then_inc(rstd3, 1)
            dve.wait_ge(rstd3, 1)
            dve.wait_ge(y_copied, 8)
            for i in range(2):
                dve.tensor_scalar(y_tok[:, 0, i * W2:(i + 1) * W2], y_tok[:, 0, i * W2:(i + 1) * W2],
                                  tok_stat[:, 2, 0:1], None, ALU.mult).then_inc(scaled[0], 1)

        @block.tensor
        def _(pe):
            def products(ph, c, t, k, act_hl):
                n, i, size = ph.slabs[k]
                s, g, q = slab_of(ph, c, t, k), group_of(ph, c, t, n), k % RING
                pe.wait_ge(lo_done, s + 1)
                if i == 0 and not (isinstance(g, int) and g < 2):
                    pe.wait_ge(evac_done, g - 1)
                b = bank(ph, n)
                for a in range(KT):
                    kt = i * KT + a
                    first, final = kt == 0, kt == size * KT - 1
                    for m in range(2):
                        dst = acc[:, b + m, 0:SEQ]
                        w_h, w_l = (w[:, q, a, m * P:(m + 1) * P] for w in (w_hi, w_lo))
                        pe.matmul(dst, w_h, act_hl[:, kt, 0, :], start=first, stop=False)
                        pe.matmul(dst, w_h, act_hl[:, kt, 1, :], start=False, stop=False)
                        last = pe.matmul(dst, w_l, act_hl[:, kt, 0, :], start=False, stop=final)
                last.then_inc(slab_used, 1)

            def transposed(dst, src):
                return pe.transpose(dst, src, ident[0:src.shape[0], 0:src.shape[0]])

            def sum_over_partitions(src_done, value, done):
                pe.wait_ge(src_done, value)
                pe.matmul(aux[2][:, 0:SEQ], ones[:, :], stat[:, :] if src_done is not fold1 else merged[:, 0, :],
                          start=True, stop=True).then_inc(done, 1)

            pe.wait_ge(consts, 2)
            pe.wait_ge(rows_g_in, 16)
            transposed(aux[3][:, PR_G1:PR_G1 + NT], rows_g[:, :]).then_inc(par_t, 1)
            for i in range(8):
                if i % 2 == 0:
                    pe.wait_ge(x_in[i // 2], 16)
                if i >= 3:
                    pe.wait_ge(x_copied, i - 2)
                for e in range(2):
                    for b in range(2):
                        last = transposed(aux[i % 3][:, e * SEQ + b * P:e * SEQ + (b + 1) * P],
                                          x_tok[:, b, (2 * i + e) * P:(2 * i + e + 1) * P])
                last.then_inc(x_t, 1)

            def parameters():
                pe.wait_ge(rows_in, 8 * 16)
                transposed(aux[3][:, 0:PR_A], rows_a[:, :])
                transposed(aux[3][:, PR_LNG:PR_LNG + PR_B], rows_b[:, :])
                for j in range(HT):
                    at = PR_DW + j * TAPS
                    last = transposed(aux[3][:, at:at + TAPS], dw_rows[:, j * P:(j + 1) * P])
                last.then_inc(par_t, 1)

            def scores(t, p):
                if p == 0:
                    pe.wait_ge(q_ready, t * 2 + 2)
                    pe.wait_ge(v_ready, t * 2 + 2)
                else:
                    pe.wait_ge(masked, t * 4 + 2)
                for e in range(2):
                    part = slice(e * HD, (e + 1) * HD)
                    for b, cols in ((0, slice(0, BLK)), (1, slice(BLK, SC))):
                        last = pe.matmul(aux[e][:, cols], q_now[part, p, b * BLK:(b + 1) * BLK],
                                         k_now[part, 0, 0:(b + 1) * BLK],
                                         start=True, stop=True)
                last.then_inc(s_ready, 1)

            def transposes(t, p):
                pe.wait_ge(norm_step, t * 12 + 6 * p + 6)
                for e in range(2):
                    for b in range(3):
                        cols = slice(b * BLK, (b + 1) * BLK)
                        last = transposed(aux[2 + e][:, cols], probs[:, p, e, cols])
                last.then_inc(t_ready, 1)

            def values(t, p):
                pe.wait_ge(t_copied, t * 4 + 2 * p + 2)
                for e in range(2):
                    at = e * SEQ
                    pe.matmul(aux[p][:, at:at + BLK], v_now[:, 0, :], probs_t[:, e, 0:BLK], start=True, stop=True)
                    pe.matmul(aux[p][:, at + BLK:at + SEQ], v_now[:, 0, :], probs_t[:, e, BLK:2 * BLK], start=True, stop=False)
                    last = pe.matmul(aux[p][:, at + BLK:at + SEQ], v_now[:, 1, :], probs_t[:, e, 2 * BLK:], start=False, stop=True)
                last.then_inc(o_ready, 1)

            OPERAND = {"B": z_ba, "C": z_c, "A": z_ba, "mix": m_hl, "down": m_hl}

            def trip(ph, c, t):
                if ph == "v tokens":
                    pe.wait_ge(evac_done, PH["kv"].group0 + 2)
                    for b in range(2):
                        for e in range(2):
                            last = transposed(aux[2][:, b * KVW + e * P:b * KVW + (e + 1) * P],
                                              pair[1][:, e, b * P:(b + 1) * P])
                    last.then_inc(v_t, 1)
                    return
                for k in range(ph.nslabs):
                    n, i, size = ph.slabs[k]
                    operand = h_hl
                    if ph.name == "glu" and isinstance(t, int) and t == 0:
                        if n == 0:
                            pe.wait_ge(h_lo, KT * (i + 1))
                        if k == 3:
                            sum_over_partitions(fold1, 4, stat1)
                        if k == 4:
                            parameters()
                    if ph.name == "B":
                        if k in (2, 4):
                            scores(t, k // 4)
                        if k in (6, 9):
                            transposes(t, k // 9)
                        if k in (8, 11):
                            values(t, k // 11)
                    if ph.name in ("B", "C", "A") and n % 2:
                        operand = OPERAND[ph.name]
                        if ph.name == "B":
                            pe.wait_ge(z_b_lo, 4)
                        elif ph.name == "C":
                            pe.wait_ge(o_step, 32)
                        else:
                            pe.wait_ge(ln_v, 27)
                    if ph.name == "C" and t * ph.nslabs + k == 22:
                        sum_over_partitions(ln_v, 4, ln_pe)
                    if ph.name == "C" and t * ph.nslabs + k == 28:
                        sum_over_partitions(ln_v, 11, ln_pe)
                    if ph.name == "mix":
                        operand = m_hl
                        pe.wait_ge(m_lo, 2 * (i + 1))
                    if ph.name == "up":
                        pe.wait_ge(r_lo, KT * (i + 1))
                        if isinstance(t, int) and t == 0 and k == 2:
                            sum_over_partitions(fold2, 1, stat2)
                    if ph.name == "down":
                        operand = m_hl
                        pe.wait_ge(hid_lo, c * 8 + 2 * (i + 1))
                        if isinstance(c, int) and c == CHUNKS - 1 and i == 2 and 2 * t + n >= 1:
                            transpose_y(2 * t + n - 1)
                    products(ph, c, t, k, operand)

            def transpose_y(j):
                pe.wait_ge(y_g, 2 * j + 2)
                if j >= 2:
                    pe.wait_ge(y_copied, j - 1)
                for e in range(2):
                    for b in range(2):
                        last = transposed(aux[j % 2][:, b * 2 * P + e * P:b * 2 * P + (e + 1) * P],
                                          pair[j % 2][:, e, b * P:(b + 1) * P])
                last.then_inc(y_t, 1)

            walk(pe, trip)
            transpose_y(7)
            pe.wait_ge(fold3, 1)
            for b in range(2):
                last = pe.matmul(aux[2][:, b:b + 1], stat[:, b * P:(b + 1) * P], ones[:, 0:1], start=True, stop=True)
            last.then_inc(stat3, 1)


_INS = ["x", "norm_mix_g", "w_in", "gate_b", "conf_dw", "conf_ln_g", "conf_ln_b", "w_conf_out", "sconv_w",
        "w_sconv_out", "sinks", "w_attn_out", "w_mix_out", "norm_ffn_g", "w_up", "w_down", "final_g"]


def kernel(**inputs):
    import numpy as np
    import concourse.bacc as bacc
    from concourse.bass_utils import run_bass_kernel_spmd

    nc = bacc.Bacc("TRN2", target_bir_lowering=False, num_devices=1)
    arrays, args = {}, []
    for name in _INS:
        a = np.ascontiguousarray(inputs[name])
        arrays[f"in_{name}"] = a
        args.append(nc.dram_tensor(f"in_{name}", a.shape, mybir.dt.from_np(a.dtype), kind="ExternalInput").ap())
    args.append(nc.dram_tensor("out_y", (1, SEQ, D), F32, kind="ExternalOutput").ap())
    build(nc, *args)
    r = run_bass_kernel_spmd(nc, [arrays], core_ids=[0])
    return r.results[0]["out_y"]
```

```python
import concourse.bass as bass
from concourse import mybir
from contextlib import ExitStack

F32 = mybir.dt.float32
F32R = mybir.dt.float32r
ACT = mybir.ActivationFunctionType
ALU = mybir.AluOpType
AX = mybir.AxisListType

P = 128
D = 2048
SEQ = 256
FF = 4 * D
NT = D // P
W2 = D // 2
HT = W2 // P
TAPS = 31
TAPS3 = 3
HD = 64
HEADS = W2 // HD
KVH = 4
KVW = KVH * HD
BLK = 128
SC = 3 * BLK
MASKED = -3.0e38
RMS_EPS = 1e-6
LN_EPS = 1e-5

COLS = 256
KT = 4
ROWS = KT * P
RING = 4
LOOKAHEAD = 3
KFULL = D // ROWS
KHALF = W2 // ROWS

C_AVAL, C_AGATE = 0, W2
C_B, C_C, C_BH = 2 * W2, 3 * W2, 4 * W2
C_Q, C_K, C_V = 5 * W2, 6 * W2, 6 * W2 + KVW
C_G = 6 * W2 + 2 * KVW

PR_GB, PR_G2, PR_GF, PR_G1 = 0, 48, 64, 80
PR_LNG, PR_LNB, PR_W3, PR_DW = 128, 136, 144, 256
PR_A, PR_B = 80, 40


class Phase:

    def __init__(self, name, trips, groups, slab0, group0):
        self.name, self.trips, self.slab0, self.group0 = name, trips, slab0, group0
        self.slabs = []
        for n, size in enumerate(groups):
            self.slabs += [(n, i, size) for i in range(size)]
        self.ngroups = len(groups)
        self.nslabs = len(self.slabs)
        assert self.nslabs % RING == 0


def plan():
    rows = [("glu", 4, [KFULL] * 2), ("short", 4, [KFULL] * 3), ("kv", 1, [KFULL] * 2),
            ("q", 2, [KFULL] * 2),
            ("B", 4, [KFULL, KHALF] * 2), ("C", 4, [KFULL, KHALF] * 2), ("A", 4, [KFULL, KHALF] * 2),
            ("mix", 4, [KFULL] * 2)]
    phases, s, g = {}, 0, 0
    for name, trips, groups in rows:
        ph = phases[name] = Phase(name, trips, groups, s, g)
        s, g = s + trips * ph.nslabs, g + trips * ph.ngroups
    for name in ("up", "down"):
        ph = phases[name] = Phase(name, 4, [KFULL] * 2, s, g)
        s, g = s + 4 * ph.nslabs, g + 4 * ph.ngroups
    return phases


PH = plan()
CHUNKS = FF // D
CHUNK_SLABS = 2 * 4 * PH["up"].nslabs
CHUNK_GROUPS = 2 * 4 * PH["up"].ngroups
TOTAL = PH["up"].slab0 + CHUNKS * CHUNK_SLABS

CONV_SHORT = dict(enumerate([2, 2, 2, 1, 2, 2, 2, 0, 1, 1, 1, 0]))
CONV_B = dict(enumerate([1, 1, 2, 1, 0, 2, 2, 1, 1, 1, 2, 1]))
AT = {"scores": (2, 4), "top": (2, 4), "exp": ((3, 3), (6, 6)), "norm": (4, 7), "transpose": (6, 9),
      "copy": (6, 9), "values": (8, 11), "out": 10}
TAPS_SHORT, TAPS_B = sum(CONV_SHORT.values()), sum(CONV_B.values())
assert TAPS_SHORT + TAPS_B == TAPS


def walk(eng, body):
    def loop(name, c=0, first=0):
        with eng.Fori(first, PH[name].trips) as t:
            body(PH[name], c, t)

    body(PH["glu"], 0, 0)
    loop("glu", first=1)
    loop("short")
    body(PH["kv"], 0, 0)
    for t in range(PH["q"].trips):
        body(PH["q"], 0, t)
    body("v tokens", 0, 0)
    loop("B")
    for t in range(PH["C"].trips):
        body(PH["C"], 0, t)
    loop("A")
    loop("mix")
    body(PH["up"], 0, 0)
    loop("up", first=1)
    loop("down")
    with eng.Fori(1, CHUNKS - 1) as c:
        loop("up", c)
        loop("down", c)
    loop("up", CHUNKS - 1)
    for t in range(PH["down"].trips):
        body(PH["down"], CHUNKS - 1, t)


def slab_of(ph, c, t, k):
    return ph.slab0 + k + t * ph.nslabs + c * CHUNK_SLABS


def group_of(ph, c, t, n):
    return ph.group0 + n + t * ph.ngroups + c * CHUNK_GROUPS


def copies(ph, c, t, n):
    return group_of(ph, 0, t, n) + 1 if ph.name != "up" else PH["mix"].group0 + n + (t + c * ph.trips) * ph.ngroups + 1


def build(nc, x, norm_mix_g, w_in, gate_b, conf_dw, conf_ln_g, conf_ln_b, w_conf_out, sconv_w,
          w_sconv_out, sinks, w_attn_out, w_mix_out, norm_ffn_g, w_up, w_down, final_g, out):
    w_in, w_conf_out, w_sconv_out = w_in[0], w_conf_out[0], w_sconv_out[0]
    w_attn_out, w_mix_out, w_up, w_down = w_attn_out[0], w_mix_out[0], w_up[0], w_down[0]

    ctx = ExitStack()
    with ctx:
        def sb(name, shape, dt=F32):
            return ctx.enter_context(nc.sbuf_tensor(name, shape, dt))

        def sem(name):
            return ctx.enter_context(nc.semaphore(name))

        w_raw = sb("w_raw", [P, RING, KT, COLS])
        w_hi = sb("w_hi", [P, RING, KT, COLS], F32R)
        w_lo = sb("w_lo", [P, RING, KT, COLS], F32R)
        res = sb("res", [P, NT, SEQ])
        h_hl = sb("h_hl", [P, NT, 2, SEQ], F32R)
        z_ba = sb("z_ba", [P, HT, 2, SEQ], F32R)
        merged = sb("merged", [P, NT, SEQ])
        PADL = TAPS - 1
        GLU_AT = HT * 2 * SEQ
        CONV_AT = GLU_AT + HT * (PADL + SEQ)
        REGION = CONV_AT + HT * SEQ
        region = sb("region", [P, REGION])

        def view(name, whole, offset, shape, dt=F32):
            return nc.alloc_sbuf_tensor_at(name, shape, dt, offset=nc.lookup_mloc(whole).addr + 4 * offset)

        z_c = view("z_c", region, 0, [P, HT, 2, SEQ], F32R)
        glu = view("glu", region, GLU_AT, [P, HT, PADL + SEQ])
        conv = view("conv", region, CONV_AT, [P, HT, SEQ])
        m_hl = view("m_hl", region, 0, [P, NT, 2, SEQ], F32R)
        x_tok = view("x_tok", region, 0, [P, 2, D])
        dw_rows = view("dw_rows", region, GLU_AT, [TAPS, W2])
        rows_g = view("rows_g", region, CONV_AT, [NT, P])
        rows_a = view("rows_a", region, CONV_AT + P, [PR_A, P])
        rows_b = view("rows_b", region, CONV_AT + 2 * P, [PR_B, P])
        y_tok = view("y_tok", merged, 0, [P, 2, D])

        q_t = sb("q_t", [P, HT, SEQ])
        k_dup = sb("k_dup", [P, KVH, SEQ])
        v_tok = sb("v_tok", [P, 2, KVW])
        pair = [sb(f"pair{i}", [P, 2, SEQ]) for i in range(3)]
        second = sb("second", [P, 2, SEQ])
        gate = sb("gate", [P, 2, SEQ])
        gated = sb("gated", [P, 2, (TAPS3 - 1) + SEQ])
        probs = sb("probs", [P, 2, 2, SC])
        probs_t = sb("probs_t", [P, 2, SC])
        q_now = sb("q_now", [P, 2, SEQ])
        k_now = sb("k_now", [P, 1, SEQ])
        v_now = sb("v_now", [P, 2, P])
        mask = sb("mask", [P, SC])
        ident = sb("ident", [P, P])
        ones = sb("ones", [P, P])
        rstd = sb("rstd", [P, SEQ])
        stat = sb("stat", [P, SEQ])
        par = sb("par", [P, 512])
        sinkb = sb("sinkb", [P, HEADS])
        top = sb("top", [P, 2, 2, 2])
        neg_top = sb("neg_top", [P, 2, 2, 2])
        sink_d = sb("sink_d", [P, 2, 2, 2])
        sink_e = sb("sink_e", [P, 2, 2, 2])
        denom = sb("denom", [P, 2, 2, 2])
        rdenom = sb("rdenom", [P, 2, 2, 2])
        tok_stat = sb("tok_stat", [P, 4, 2])

        acc = ctx.enter_context(nc.psum_tensor("acc", [P, 8, 512], F32))
        aux = [acc[:, 4 + i, :] for i in range(4)]

        raw_full = [sem(f"raw_full{i}") for i in range(RING)]
        hi_done, lo_done, slab_used = sem("hi_done"), sem("lo_done"), sem("slab_used")
        half_copied, half_sum, evac_done = sem("half_copied"), sem("half_sum"), sem("evac_done")
        zeroed, consts, par_t, par_ok = sem("zeroed"), sem("consts"), sem("par_t"), sem("par_ok")
        warm, rows_g_in, rows_in = sem("warm"), sem("rows_g_in"), sem("rows_in")
        x_in = [sem(f"x_in{i}") for i in range(4)]
        x_t, x_copied, x_hi, x_hi2, h_lo, x_sq = (sem(n) for n in ("x_t", "x_copied", "x_hi", "x_hi2", "h_lo", "x_sq"))
        fold1, stat1, var1, root1, rstd1 = sem("fold1"), sem("stat1"), sem("var1"), sem("root1"), sem("rstd1")
        glu_sig, glu_done, gated_done, short_step, z_b_f, z_b_hi, z_b_lo = (sem(n) for n in (
            "glu_sig", "glu_done", "gated_done", "short_step", "z_b_f", "z_b_hi", "z_b_lo"))
        conv_a, conv_b, conv_c = sem("conv_a"), sem("conv_b"), sem("conv_c")
        k_in, v_t, v_copied = sem("k_in"), sem("v_t"), sem("v_copied")
        q_ready, v_ready, s_ready, masked, top_step, exp_done, norm_step, t_ready, t_copied, o_ready, o_step = (
            sem(n) for n in ("q_ready", "v_ready", "s_ready", "masked", "top_step", "exp_done", "norm_step",
                             "t_ready", "t_copied", "o_ready", "o_step"))
        ln_v, ln_pe, ln_act = sem("ln_v"), sem("ln_pe"), sem("ln_act")
        gate_sig, m_sum, m_hi, m_lo = sem("gate_sig"), sem("m_sum"), sem("m_hi"), sem("m_lo")
        r_hi, r_sq, r_lo, r_sum = sem("r_hi"), sem("r_sq"), sem("r_lo"), sem("r_sum")
        fold2, stat2, var2, root2, rstd2 = sem("fold2"), sem("stat2"), sem("var2"), sem("root2"), sem("rstd2")
        hid_f, hid_hi, hid_lo = sem("hid_f"), sem("hid_hi"), sem("hid_lo")
        y_g, y_sq, y_t, y_copied, y_sum = sem("y_g"), sem("y_sq"), sem("y_t"), sem("y_copied"), sem("y_sum")
        fold3, stat3, var3, root3, rstd3, stored = (sem(n) for n in (
            "fold3", "stat3", "var3", "root3", "rstd3", "stored"))

        scaled = [sem("scaled0"), sem("scaled1")]

        block = ctx.enter_context(nc.Block())

        def both(t2):
            return t2[:, None, :].to_broadcast((P, 2, SEQ))

        def bank(ph, n):
            return 2 * n if ph.ngroups == 3 else 2 * (n % 2)

        @block.sync
        def _(sp):
            def load_x(i):
                cols = slice(i * D // 4, (i + 1) * D // 4)
                sp.dma_start(x_tok[:, :, cols], x[0][:, cols].rearrange("(b p) n -> p b n", p=P)).then_inc(x_in[i], 16)

            def load_slab(ph, c, t, k):
                n, i, _ = ph.slabs[k]
                s = slab_of(ph, c, t, k)
                if ph.name in ("B", "C", "A"):
                    b = {"A": 0, "B": 1, "C": 2}[ph.name]
                    col = t * (2 * COLS) + (n // 2) * COLS
                    if n % 2:
                        w = (w_conf_out, w_sconv_out, w_attn_out)[b]
                    else:
                        w, col = w_in, col + (C_G + b * D)
                    row = i * ROWS
                else:
                    w, starts = {"glu": (w_in, (C_AVAL, C_AGATE)), "short": (w_in, (C_C, C_BH, C_B)),
                                 "kv": (w_in, (C_K, C_V)), "q": (w_in, (C_Q, C_Q + COLS)),
                                 "mix": (w_mix_out, (0, COLS)), "up": (w_up, (0, COLS)),
                                 "down": (w_down, (0, COLS))}[ph.name]
                    step = COLS * (1 if ph.name in ("glu", "short") else 2)
                    col = t * step + starts[n]
                    row = i * ROWS
                    if ph.name == "up":
                        col = c * D + col
                    if ph.name == "down":
                        row = c * D + row
                shared = ph.name in ("B", "A")
                if not (isinstance(s, int) and s < RING or shared and k == 4):
                    sp.wait_ge(lo_done, s + (shared and k == 3) - (RING - 1))
                sp.dma_start(w_raw[:, k % RING], w[bass.ds(row, ROWS), bass.ds(col, COLS)]
                             .rearrange("(a p) n -> p a n", p=P)).then_inc(raw_full[k % RING], 16)

            def trip(ph, c, t):
                if ph == "v tokens":
                    return
                for k in range(ph.nslabs):
                    if ph.name == "glu" and isinstance(t, int) and t == 0 and k == 1:
                        load_x(2)
                        load_x(3)
                    if ph.name == "glu" and isinstance(t, int) and t == 0 and k == 3:
                        load_rows()
                    if ph.name == "q" and k == 2 and t == 0:
                        sp.wait_ge(evac_done, PH["kv"].group0 + 1)
                        for half in range(2):
                            for odd in range(2):
                                sp.dma_start(k_dup[half * HD:(half + 1) * HD, odd:KVH:2, :],
                                             pair[0][odd * HD:(odd + 1) * HD, :, :]).then_inc(k_in, 16)
                    load_slab(ph, c, t, k)

            def rows(dst, src, done):
                sp.dma_start(dst, src).then_inc(done, 16)

            def load_rows():
                rows(rows_a[0:48, :], gate_b[0].rearrange("b (t p) -> (b t) p", p=P), rows_in)
                rows(rows_a[48:64, :], norm_ffn_g[0].rearrange("(t p) -> t p", p=P), rows_in)
                rows(rows_a[64:80, :], final_g.rearrange("(t p) -> t p", p=P), rows_in)
                rows(rows_b[0:8, :], conf_ln_g[0].rearrange("(t p) -> t p", p=P), rows_in)
                rows(rows_b[8:16, :], conf_ln_b[0].rearrange("(t p) -> t p", p=P), rows_in)
                rows(rows_b[16:40, :], sconv_w[0].rearrange("k (t p) -> (k t) p", p=P), rows_in)
                rows(dw_rows[:, :], conf_dw[0], rows_in)
                rows(sinkb[:, :], sinks.to_broadcast((P, HEADS)), rows_in)

            rows(rows_g[:, :], norm_mix_g[0].rearrange("(t p) -> t p", p=P), rows_g_in)
            load_x(0)
            load_x(1)
            walk(sp, trip)
            for i in range(4):
                b, cols = i % 2, slice((i // 2) * W2, (i // 2 + 1) * W2)
                sp.wait_ge(scaled[b], i // 2 + 1)
                sp.dma_start(out[0][b * P:(b + 1) * P, cols], y_tok[:, b, cols]).then_inc(stored, 16)
            sp.wait_ge(stored, 64)

        @block.gpsimd
        def _(pool):
            pool.memset(ident[:, :], 0.0).then_inc(zeroed, 1)
            pool.memset(ones[:, :], 1.0).then_inc(consts, 1)
            pool.wait_ge(zeroed, 1)
            pool.affine_select(out=ident[:, :], in_=ident[:, :], compare_op=ALU.not_equal, fill=1.0, base=0,
                               pattern=[[-1, P]], channel_multiplier=1).then_inc(consts, 1)
            pool.memset(mask[:, :], 0.0).then_inc(zeroed, 1)
            pool.wait_ge(zeroed, 2)
            for lo in (0, 2 * BLK):
                pool.affine_select(out=mask[:, lo:lo + BLK], in_=mask[:, lo:lo + BLK], compare_op=ALU.is_ge,
                                   fill=MASKED, base=0, pattern=[[-1, BLK]], channel_multiplier=1).then_inc(consts, 1)
            pool.affine_select(out=mask[:, BLK:2 * BLK], in_=mask[:, BLK:2 * BLK], compare_op=ALU.is_ge,
                               fill=MASKED, base=-1, pattern=[[1, BLK]], channel_multiplier=-1).then_inc(consts, 1)

            def square(i):
                pool.wait_ge(x_copied, i + 1)
                tiles = slice(2 * i, 2 * i + 2)
                pool.tensor_tensor(merged[:, tiles, :], res[:, tiles, :], res[:, tiles, :], ALU.mult).then_inc(x_sq, 1)

            def add(i):
                pool.wait_ge(x_sq, i + 1)
                if i >= 2:
                    pool.wait_ge(fold1, i - 1)
                pool.tensor_tensor(merged[:, 0:2, :], merged[:, 0:2, :], merged[:, 2 * i:2 * i + 2, :],
                                   ALU.add).then_inc(fold1, 1)

            square(0)
            for i in range(1, 8):
                square(i)
                if i >= 2:
                    add(i - 1)
            add(7)
            pool.wait_ge(fold1, 7)
            pool.tensor_tensor(merged[:, 0, :], merged[:, 0, :], merged[:, 1, :], ALU.add).then_inc(fold1, 1)

        @block.scalar
        def _(act):
            def hi(ph, c, t, k):
                s = slab_of(ph, c, t, k)
                if isinstance(s, int) and s + LOOKAHEAD >= TOTAL:
                    return
                ahead = k + LOOKAHEAD
                act.wait_ge(raw_full[ahead % RING], 16 * (ph.slab0 // RING + ahead // RING + 1)
                            + t * (16 * ph.nslabs // RING) + c * (16 * CHUNK_SLABS // RING))
                if not (isinstance(s, int) and s == 0):
                    act.wait_ge(slab_used, s)
                act.activation(w_hi[:, ahead % RING], w_raw[:, ahead % RING], ACT.Copy).then_inc(hi_done, 1)

            def start_pair(i):
                act.wait_ge(x_t, i + 1)
                act.activation(res[:, 2 * i:2 * i + 2, :], aux[i % 3][:, :].rearrange("p (e n) -> p e n", e=2),
                               ACT.Copy).then_inc(x_copied, 1)
                act.wait_ge(x_copied, i + 1)
                act.activation(h_hl[:, 2 * i, 0, :], res[:, 2 * i, :], ACT.Copy,
                               scale=par[:, PR_G1 + 2 * i:PR_G1 + 2 * i + 1]).then_inc(x_hi, 1)

            def prologue(s):
                act.wait_ge(raw_full[s], 16)
                act.activation(w_hi[:, s], w_raw[:, s], ACT.Copy).then_inc(hi_done, 1)

            act.wait_ge(consts, 1)
            act.activation(tok_stat[:, 1, 0:1], ones[:, 0:1], ACT.Sqrt).then_inc(warm, 1)
            act.wait_ge(par_ok, 1)
            for i in range(8):
                start_pair(i)
                if i in (1, 3, 5):
                    prologue(i // 2)

            def gates(ph, t, n, b):
                g = group_of(ph, 0, t, n)
                act.wait_ge(evac_done, g + 1)
                for e in range(2):
                    col = t * 4 + (PR_GB + b * NT + n + e)
                    act.activation(gate[:, e, :], pair[0][:, e, :], ACT.Sigmoid,
                                   bias=par[:, bass.ds(col, 1)]).then_inc(gate_sig, 1)

            def exps(t, p, e):
                act.wait_ge(top_step, t * 10 + 5 * p + 5)
                for b, cols in ((0, slice(0, BLK)), (1, slice(BLK, SC))):
                    act.activation(probs[:, p, e, cols], probs[:, p, e, cols], ACT.Exp,
                                   bias=neg_top[:, p, e, b:b + 1],
                                   accum_out=denom[:, p, e, b:b + 1]).then_inc(exp_done, 1)
                if e == 1:
                    act.activation(sink_e[:, p], sink_d[:, p], ACT.Exp).then_inc(exp_done, 1)

            def copy_t(t, p):
                act.wait_ge(t_ready, t * 2 + p + 1)
                if p == 1:
                    act.wait_ge(o_ready, t * 2 + 1)
                for e in range(2):
                    act.activation(probs_t[:, e, :], aux[2 + e][:, 0:SC], ACT.Copy).then_inc(t_copied, 1)

            def ln_square(i):
                act.wait_ge(ln_v, 6 + i)
                act.activation(glu[:, 4 * i:4 * i + 4, 0:SEQ], conv[:, 4 * i:4 * i + 4, :], ACT.Square).then_inc(ln_act, 1)

            def ln_root():
                act.wait_ge(ln_v, 12)
                act.activation(stat[:, :], stat[:, :], ACT.Sqrt).then_inc(ln_act, 1)

            def ln_sigmoid(part):
                for j in range(4 * part, 4 * part + 4):
                    act.wait_ge(ln_v, 14 + j)
                    act.activation(glu[:, j, 0:SEQ], conv[:, j, :], ACT.Sigmoid,
                                   bias=par[:, PR_LNB + j:PR_LNB + j + 1]).then_inc(ln_act, 1)

            def ln_hi(i):
                act.wait_ge(ln_v, 25 + 4 * i)
                act.activation(z_ba[:, 4 * i:4 * i + 4, 0, :], conv[:, 4 * i:4 * i + 4, :], ACT.Copy).then_inc(ln_act, 1)

            LN = {30: (ln_square, 0), 31: (ln_square, 1), 36: (ln_root,), 39: (ln_sigmoid, 0), 41: (ln_sigmoid, 1),
                  43: (ln_hi, 0), 44: (ln_hi, 1)}

            def trip(ph, c, t):
                if ph == "v tokens":
                    return
                for k in range(ph.nslabs):
                    hi(ph, c, t, k)
                    n, i, size = ph.slabs[k]
                    ends = i == size - 1
                    g = group_of(ph, c, t, n)
                    if ph.name == "B":
                        if k == 0:
                            act.wait_ge(evac_done, PH["q"].group0 + 4)
                            act.activation(q_now[:, :, :], q_t[:, bass.ds(t * 2, 2), :], ACT.Copy,
                                           scale=float(HD) ** -0.5).then_inc(q_ready, 1)
                            act.wait_ge(k_in, 64)
                            act.activation(k_now[:, :, :], k_dup[:, bass.ds(t, 1), :], ACT.Copy).then_inc(q_ready, 1)
                        for p in range(2):
                            if k == AT["copy"][p]:
                                copy_t(t, p)
                            for e in range(2):
                                if k == AT["exp"][p][e]:
                                    exps(t, p, e)
                    if ends and ph.name not in ("mix", "down"):
                        act.wait_ge(slab_used, slab_of(ph, c, t, k) + 1)
                        if not (isinstance(g, int) and g == 0):
                            act.wait_ge(half_sum, g)
                        b = bank(ph, n)
                        act.activation(second[:, :, :], acc[:, b:b + 2, SEQ:], ACT.Copy).then_inc(half_copied, 1)
                    if ph.name == "glu":
                        if isinstance(t, int) and t == 0 and k == 5:
                            act.wait_ge(var1, 1)
                            act.activation(rstd[:, :], stat[:, :], ACT.Sqrt).then_inc(root1, 1)
                        if ends and n == 1:
                            act.wait_ge(evac_done, g + 1)
                            act.activation(gate[:, :, :], pair[1][:, :, :], ACT.Sigmoid).then_inc(glu_sig, 1)
                    if ph.name == "short" and ends and n == 2:
                        act.wait_ge(z_b_f, t + 1)
                        act.activation(z_ba[:, bass.ds(t * 2, 2), 0, :], pair[2][:, :, :], ACT.Copy).then_inc(z_b_hi, 1)
                    if ph.name in ("B", "C", "A") and n % 2 and i == 0:
                        gates(ph, t, n - 1, {"A": 0, "B": 1, "C": 2}[ph.name])
                    if ph.name == "C" and t * ph.nslabs + k in LN:
                        step, *part = LN[t * ph.nslabs + k]
                        step(*part)
                    if ph.name == "A" and ends and n % 2 == 1:
                        j = t * 2 + n // 2
                        act.wait_ge(m_sum, j + 9)
                        act.activation(m_hl[:, bass.ds(j * 2, 2), 0, :], merged[:, bass.ds(j * 2, 2), :],
                                       ACT.Copy).then_inc(m_hi, 1)
                    if ph.name == "mix" and ends:
                        j = t * 2 + n
                        act.wait_ge(evac_done, g + 1)
                        for e in range(2):
                            act.activation(h_hl[:, bass.ds(j * 2 + e, 1), 0, :], res[:, bass.ds(j * 2 + e, 1), :], ACT.Copy,
                                           scale=par[:, bass.ds(j * 2 + (PR_G2 + e), 1)]).then_inc(r_hi, 1)
                        act.activation(pair[n][:, :, :], res[:, bass.ds(j * 2, 2), :], ACT.Square).then_inc(r_sq, 1)
                    if ph.name == "up":
                        if isinstance(t, int) and t == 0 and k == 2:
                            act.wait_ge(var2, 1)
                            act.activation(rstd[:, :], stat[:, :], ACT.Sqrt).then_inc(root2, 1)
                        if ends:
                            j = t * 2 + n
                            act.wait_ge(hid_f, c * 8 + j + 1)
                            act.activation(m_hl[:, bass.ds(j * 2, 2), 0, :], pair[n][:, :, :], ACT.Copy).then_inc(hid_hi, 1)
                    if ph.name == "down" and isinstance(c, int) and c == CHUNKS - 1 and ends:
                        j = 2 * t + n
                        act.wait_ge(evac_done, g + 1)
                        if j >= 2:
                            act.wait_ge(y_sum, j - 1)
                        act.activation((pair[2], gate)[n][:, :, :], res[:, 2 * j:2 * j + 2, :], ACT.Square).then_inc(y_sq, 1)
                        if j >= 2:
                            act.wait_ge(y_t, j - 1)
                        for e in range(2):
                            act.activation(pair[n][:, e, :], res[:, 2 * j + e, :], ACT.Copy,
                                           scale=par[:, PR_GF + 2 * j + e:PR_GF + 2 * j + e + 1]).then_inc(y_g, 1)

            walk(act, trip)
            act.wait_ge(var3, 1)
            act.activation(tok_stat[:, 1, :], tok_stat[:, 0, :], ACT.Sqrt).then_inc(root3, 1)
            act.wait_ge(rstd3, 1)
            act.wait_ge(y_copied, 8)
            for i in range(2):
                act.activation(y_tok[:, 1, i * W2:(i + 1) * W2], y_tok[:, 1, i * W2:(i + 1) * W2], ACT.Copy,
                               scale=tok_stat[:, 2, 1:2]).then_inc(scaled[1], 1)

        @block.vector
        def _(dve):
            def lo(ph, c, t, k):
                s = slab_of(ph, c, t, k)
                if isinstance(s, int) and s + LOOKAHEAD >= TOTAL:
                    return
                q = (k + LOOKAHEAD) % RING
                dve.wait_ge(hi_done, s + (LOOKAHEAD + 1))
                dve.tensor_tensor(w_lo[:, q], w_raw[:, q], w_hi[:, q].bitcast(F32), ALU.subtract).then_inc(lo_done, 1)

            def prologue(s):
                dve.wait_ge(hi_done, s + 1)
                dve.tensor_tensor(w_lo[:, s], w_raw[:, s], w_hi[:, s].bitcast(F32), ALU.subtract).then_inc(lo_done, 1)

            def start_pair(i):
                tiles = (2 * i + 1, 2 * i)
                gain = [par[:, PR_G1 + tile:PR_G1 + tile + 1] for tile in tiles]
                dve.wait_ge(x_copied, i + 1)
                dve.tensor_scalar(h_hl[:, tiles[0], 0, :], res[:, tiles[0], :], gain[0], None, ALU.mult).then_inc(x_hi2, 1)
                dve.wait_ge(x_hi, i + 1)
                dve.wait_ge(x_hi2, i + 1)
                for tile, g in zip(tiles, gain):
                    dve.scalar_tensor_tensor(h_hl[:, tile, 1, :], res[:, tile, :], g, h_hl[:, tile, 0, :].bitcast(F32),
                                             ALU.mult, ALU.subtract).then_inc(h_lo, 1)

            dve.wait_ge(par_t, 1)
            dve.tensor_copy(par[:, PR_G1:PR_G1 + NT], aux[3][:, PR_G1:PR_G1 + NT]).then_inc(par_ok, 1)
            dve.wait_ge(par_ok, 1)
            for i in range(8):
                start_pair(i)
                if i in (1, 3, 5):
                    prologue(i // 2)

            def parameters():
                dve.memset(gated[:, :, 0:TAPS3 - 1], 0.0).then_inc(par_ok, 1)
                dve.wait_ge(par_t, 2)
                dve.tensor_copy(par[:, 0:PR_A], aux[3][:, 0:PR_A]).then_inc(par_ok, 1)
                dve.tensor_copy(par[:, PR_LNG:PR_LNG + PR_B], aux[3][:, PR_LNG:PR_LNG + PR_B]).then_inc(par_ok, 1)
                dve.tensor_copy(par[:, PR_DW:PR_DW + HT * TAPS], aux[3][:, PR_DW:PR_DW + HT * TAPS]).then_inc(par_ok, 1)
                dve.memset(glu[:, :, 0:PADL], 0.0).then_inc(par_ok, 1)

            def mean_eps(dst, src, scale, eps, done):
                dve.tensor_scalar(dst, src, scale, eps, ALU.mult, ALU.add).then_inc(done, 1)

            def tap(tile, k, step, at):
                w = par[:, bass.ds(tile * TAPS + (PR_DW + k), 1)]
                src = glu[:, bass.ds(tile, 1), k:k + SEQ]
                dst = conv[:, bass.ds(tile, 1), :]
                if k == 0:
                    dve.tensor_scalar(dst, src, w, None, ALU.mult).then_inc(step, 1)
                else:
                    if at is not None:
                        dve.wait_ge(step, at)
                    dve.scalar_tensor_tensor(dst, src, w, dst, ALU.mult, ALU.add).then_inc(step, 1)

            def top_of(t, p):
                dve.wait_ge(s_ready, t * 2 + p + 1)
                for e in range(2):
                    dve.tensor_tensor(probs[:, p, e, :], aux[e][:, 0:SC], mask[:, :], ALU.add).then_inc(masked, 1)
                dve.wait_ge(masked, t * 4 + 2 * p + 2)
                dve.reduce_max(top[:, p, :, 0], probs[:, p, :, 0:BLK], AX.X).then_inc(top_step, 1)
                dve.reduce_max(top[:, p, :, 1], probs[:, p, :, BLK:SC], AX.X).then_inc(top_step, 1)
                dve.wait_ge(top_step, t * 10 + 5 * p + 2)
                sink = sinkb[:, bass.ds(t * 4 + 2 * p, 2)][:, :, None].to_broadcast((P, 2, 2))
                dve.tensor_tensor(top[:, p], top[:, p], sink, ALU.max).then_inc(top_step, 1)
                dve.wait_ge(top_step, t * 10 + 5 * p + 3)
                dve.tensor_scalar(neg_top[:, p], top[:, p], -1.0, None, ALU.mult).then_inc(top_step, 1)
                dve.tensor_tensor(sink_d[:, p], sink, top[:, p], ALU.subtract).then_inc(top_step, 1)

            def normalise(t, p):
                dve.wait_ge(exp_done, t * 10 + 5 * p + 5)
                dve.tensor_tensor(denom[:, p], denom[:, p], sink_e[:, p], ALU.add).then_inc(norm_step, 1)
                dve.wait_ge(norm_step, t * 12 + 6 * p + 1)
                dve.reciprocal(rdenom[:, p], denom[:, p]).then_inc(norm_step, 1)
                dve.wait_ge(norm_step, t * 12 + 6 * p + 2)
                for e in range(2):
                    for b, cols in ((0, slice(0, BLK)), (1, slice(BLK, SC))):
                        dve.tensor_scalar(probs[:, p, e, cols], probs[:, p, e, cols], rdenom[:, p, e, b:b + 1], None,
                                          ALU.mult).then_inc(norm_step, 1)

            def head_out(t, p):
                dve.wait_ge(o_ready, t * 2 + p + 1)
                j = t * 2 + p
                for e in range(2):
                    part = slice(e * HD, (e + 1) * HD)
                    dve.tensor_copy(z_c[part, bass.ds(j, 1), 0, :], aux[p][part, None, e * SEQ:(e + 1) * SEQ]).then_inc(o_step, 1)
                dve.wait_ge(o_step, t * 8 + 4 * p + 2)
                for e in range(2):
                    part = slice(e * HD, (e + 1) * HD)
                    dve.tensor_tensor(z_c[part, bass.ds(j, 1), 1, :], aux[p][part, None, e * SEQ:(e + 1) * SEQ],
                                      z_c[part, bass.ds(j, 1), 0, :].bitcast(F32), ALU.subtract).then_inc(o_step, 1)

            def ln_fold(src, base, part):
                steps = ((pair[2][:, :, :], src(0, 2), src(2, 4)), (pair[1][:, :, :], src(4, 6), src(6, 8)),
                         (pair[2][:, :, :], pair[2][:, :, :], pair[1][:, :, :]),
                         (stat[:, :], pair[2][:, 0, :], pair[2][:, 1, :]))
                for n in (2 * part, 2 * part + 1):
                    if n >= 2:
                        dve.wait_ge(ln_v, base + n)
                    dve.tensor_tensor(*steps[n], ALU.add).then_inc(ln_v, 1)

            def ln_sum(part):
                if part == 0:
                    dve.wait_ge(conv_b, 4 * TAPS_B)
                    dve.wait_ge(conv_c, 4 * TAPS)
                    dve.wait_ge(m_sum, 4)
                ln_fold(lambda a, b: conv[:, a:b, :], 0, part)

            def ln_center(part):
                if part == 0:
                    dve.wait_ge(ln_pe, 1)
                    mean_eps(stat[:, :], aux[2][:, 0:SEQ], 1.0 / W2, 0.0, ln_v)
                    dve.wait_ge(ln_v, 5)
                tiles = slice(4 * part, 4 * part + 4)
                dve.tensor_tensor(conv[:, tiles, :], conv[:, tiles, :],
                                  stat[:, None, :].to_broadcast((P, 4, SEQ)), ALU.subtract).then_inc(ln_v, 1)

            def ln_sum2(part):
                if part == 0:
                    dve.wait_ge(ln_act, 2)
                    dve.wait_ge(m_sum, 5)
                ln_fold(lambda a, b: glu[:, a:b, 0:SEQ], 7, part)

            def ln_var():
                dve.wait_ge(ln_pe, 2)
                mean_eps(stat[:, :], aux[2][:, 0:SEQ], 1.0 / W2, LN_EPS, ln_v)

            def ln_rstd():
                dve.wait_ge(ln_act, 3)
                dve.reciprocal(stat[:, :], stat[:, :]).then_inc(ln_v, 1)

            def ln_norm(part):
                dve.wait_ge(ln_v, 13)
                for j in range(4 * part, 4 * part + 4):
                    dve.scalar_tensor_tensor(conv[:, j, :], conv[:, j, :], par[:, PR_LNG + j:PR_LNG + j + 1],
                                             stat[:, :], ALU.mult, ALU.mult).then_inc(ln_v, 1)

            def ln_silu(part):
                for j in range(4 * part, 4 * part + 4):
                    dve.wait_ge(ln_act, 4 + j)
                    dve.scalar_tensor_tensor(conv[:, j, :], conv[:, j, :], par[:, PR_LNB + j:PR_LNB + j + 1],
                                             glu[:, j, 0:SEQ], ALU.add, ALU.mult).then_inc(ln_v, 1)

            def ln_lo(part):
                dve.wait_ge(ln_act, 12 + part)
                tiles = slice(4 * part, 4 * part + 4)
                dve.tensor_tensor(z_ba[:, tiles, 1, :], conv[:, tiles, :],
                                  z_ba[:, tiles, 0, :].bitcast(F32), ALU.subtract).then_inc(ln_v, 1)

            LN = {24: (ln_sum, 0), 25: (ln_sum, 1), 28: (ln_center, 0), 30: (ln_center, 1), 32: (ln_sum2, 0),
                  34: (ln_sum2, 1), 36: (ln_var,), 37: (ln_rstd,), 38: (ln_norm, 0), 40: (ln_norm, 1),
                  42: (ln_silu, 0), 43: (ln_silu, 1), 44: (ln_lo, 0), 46: (ln_lo, 1)}

            taps_c = [(tile0 + e, k) for tile0 in (4, 6) for k in range(TAPS) for e in range(2)]
            done_c = [0]

            def taps_static(n):
                for tile, k in taps_c[done_c[0]:done_c[0] + n]:
                    tap(tile, k, conv_c, done_c[0] - 1)
                    done_c[0] += 1

            def taps_b(t, k, part):
                if CONV_B[k] > part:
                    m = TAPS_SHORT + part + sum(CONV_B[m] for m in range(k))
                    if m == TAPS_SHORT:
                        dve.wait_ge(conv_a, 4 * TAPS_SHORT)
                    tap(t, m, conv_b, None if m == TAPS_SHORT else t * TAPS_B + (m - TAPS_SHORT))

            def trip(ph, c, t):
                if ph == "v tokens":
                    dve.wait_ge(v_t, 1)
                    dve.tensor_copy(v_tok[:, :, :].rearrange("p b n -> p (b n)"), aux[2][:, :]).then_inc(v_copied, 1)
                    return
                for k in range(ph.nslabs):
                    if ph.name == "B":
                        for p in range(2):
                            if k == AT["norm"][p]:
                                normalise(t, p)
                        if k == 0:
                            dve.wait_ge(v_copied, 1)
                            dve.wait_ge(consts, 5)
                            for half in range(2):
                                dve.tensor_copy(v_now[:, :, half * HD:(half + 1) * HD],
                                                v_tok[:, :, bass.ds(t * HD, HD)]).then_inc(v_ready, 1)
                        taps_b(t, k, 0)
                    lo(ph, c, t, k)
                    n, i, size = ph.slabs[k]
                    s, g, ends = slab_of(ph, c, t, k), group_of(ph, c, t, n), i == size - 1
                    if ph.name == "glu" and isinstance(t, int) and t == 0:
                        if k == 3:
                            dve.wait_ge(stat1, 1)
                            mean_eps(stat[:, :], aux[2][:, 0:SEQ], 1.0 / D, RMS_EPS, var1)
                            dve.wait_ge(root1, 1)
                            dve.reciprocal(rstd[:, :], rstd[:, :]).then_inc(rstd1, 1)
                            dve.wait_ge(rstd1, 1)
                        if k == 5:
                            parameters()
                    if ph.name == "up" and isinstance(t, int) and t == 0:
                        if k == 0:
                            dve.wait_ge(r_sum, 9)
                            dve.tensor_tensor(stat[:, :], pair[2][:, 0, :], pair[2][:, 1, :], ALU.add).then_inc(fold2, 1)
                        if k == 1:
                            dve.wait_ge(stat2, 1)
                            mean_eps(stat[:, :], aux[2][:, 0:SEQ], 1.0 / D, RMS_EPS, var2)
                        if k == 2:
                            dve.wait_ge(root2, 1)
                            dve.reciprocal(rstd[:, :], rstd[:, :]).then_inc(rstd2, 1)
                            dve.wait_ge(rstd2, 1)
                    if ph.name == "short":
                        if k == 0:
                            dve.wait_ge(glu_done, 4)
                            dve.wait_ge(par_ok, 6)
                        first = sum(CONV_SHORT[m] for m in range(k))
                        for m in range(first, first + CONV_SHORT[k]):
                            tap(t, m, conv_a, t * TAPS_SHORT + m)
                        if k in (8, 9, 10):
                            m = k - 8
                            for e in range(2):
                                src = gated[:, e, m:m + SEQ]
                                w = par[:, bass.ds(t * 2 + (PR_W3 + m * HT + e), 1)]
                                if m == 0:
                                    dve.wait_ge(gated_done, t + 1)
                                    dve.tensor_scalar(pair[1][:, e, :], src, w, None, ALU.mult).then_inc(short_step, 1)
                                else:
                                    dve.wait_ge(short_step, t * 6 + (2 * (m - 1) + e + 1))
                                    dve.scalar_tensor_tensor(pair[1][:, e, :], src, w, pair[1][:, e, :], ALU.mult,
                                                             ALU.add).then_inc(short_step, 1)
                    if ph.name == "kv":
                        taps_static(3 if not ends else 2)
                    if ph.name == "q":
                        taps_static(3 if not ends else 2)
                    if ph.name == "B":
                        for p in range(2):
                            if k == AT["top"][p]:
                                top_of(t, p)
                        if k == AT["out"]:
                            head_out(t, 0)
                        taps_b(t, k, 1)
                    if ph.name == "C":
                        at = t * ph.nslabs + k
                        if at < 24:
                            taps_static(3 if not ends else 2)
                        if at in LN:
                            step, *part = LN[at]
                            step(*part)
                    if not ends:
                        continue
                    dve.wait_ge(slab_used, s + 1)
                    halves = [acc[:, bank(ph, n):bank(ph, n) + 2, i * SEQ:(i + 1) * SEQ] for i in range(2)]

                    def total(dst, scale):
                        dve.wait_ge(half_copied, copies(ph, c, t, n))
                        dve.tensor_tensor(dst, halves[0], second[:, :, :], ALU.add).then_inc(half_sum, 1)
                        dve.wait_ge(half_sum, g + 1)
                        dve.tensor_tensor(dst, dst, scale, ALU.mult).then_inc(evac_done, 1)

                    def add_total(dst):
                        dve.tensor_tensor(dst, halves[0], dst, ALU.add).then_inc(half_sum, 1)
                        dve.wait_ge(half_sum, g + 1)
                        dve.tensor_tensor(dst, halves[1], dst, ALU.add).then_inc(evac_done, 1)

                    if ph.name in ("glu", "kv"):
                        total(pair[n][:, :, :], both(rstd))
                        if ph.name == "glu" and n == 1:
                            dve.wait_ge(glu_sig, t + 1)
                            dve.tensor_tensor(glu[:, bass.ds(t * 2, 2), PADL:PADL + SEQ], pair[0][:, :, :],
                                              gate[:, :, :], ALU.mult).then_inc(glu_done, 1)
                    elif ph.name == "short":
                        total(pair[n][:, :, :], both(rstd))
                        dve.wait_ge(evac_done, g + 1)
                        if n == 1:
                            dve.tensor_tensor(gated[:, :, TAPS3 - 1:], pair[0][:, :, :], pair[1][:, :, :],
                                              ALU.mult).then_inc(gated_done, 1)
                        if n == 2:
                            dve.wait_ge(short_step, t * 6 + 6)
                            dve.tensor_tensor(pair[2][:, :, :], pair[2][:, :, :], pair[1][:, :, :], ALU.mult).then_inc(z_b_f, 1)
                            dve.wait_ge(z_b_hi, t + 1)
                            dve.tensor_tensor(z_ba[:, bass.ds(t * 2, 2), 1, :], pair[2][:, :, :],
                                              z_ba[:, bass.ds(t * 2, 2), 0, :].bitcast(F32), ALU.subtract).then_inc(z_b_lo, 1)
                    elif ph.name == "q":
                        j = t * 2 + n
                        total(q_t[:, 2 * j:2 * j + 2, :], both(rstd))
                    elif ph.name in ("B", "C", "A") and n % 2 == 0:
                        total(pair[0][:, :, :], both(rstd))
                    elif ph.name in ("B", "C", "A"):
                        j = t * 2 + n // 2
                        first = {"B": 0, "C": 16, "A": 32}[ph.name]
                        dve.wait_ge(gate_sig, j * 2 + (first + 2))
                        m = merged[:, bass.ds(j * 2, 2), :]
                        if ph.name == "B":
                            total(m, gate[:, :, :])
                            if n == 3:
                                head_out(t, 1)
                        else:
                            total(pair[1][:, :, :], gate[:, :, :])
                            dve.wait_ge(evac_done, g + 1)
                            dve.tensor_tensor(m, m, pair[1][:, :, :], ALU.add).then_inc(m_sum, 1)
                        if ph.name == "A":
                            dve.wait_ge(m_hi, j + 1)
                            dve.tensor_tensor(m_hl[:, bass.ds(j * 2, 2), 1, :], m,
                                              m_hl[:, bass.ds(j * 2, 2), 0, :].bitcast(F32), ALU.subtract).then_inc(m_lo, 1)
                    elif ph.name == "mix":
                        j = t * 2 + n
                        r = res[:, bass.ds(j * 2, 2), :]
                        add_total(r)
                        for e in range(2):
                            dve.wait_ge(r_hi, j * 2 + (e + 1))
                            dve.scalar_tensor_tensor(h_hl[:, bass.ds(j * 2 + e, 1), 1, :], res[:, bass.ds(j * 2 + e, 1), :],
                                                     par[:, bass.ds(j * 2 + (PR_G2 + e), 1)],
                                                     h_hl[:, bass.ds(j * 2 + e, 1), 0, :].bitcast(F32),
                                                     ALU.mult, ALU.subtract).then_inc(r_lo, 1)
                        dve.wait_ge(r_sq, j + 1)
                        dve.wait_ge(r_sum, j + 1)
                        dve.tensor_tensor(pair[2][:, :, :], pair[2][:, :, :], pair[n][:, :, :], ALU.add).then_inc(r_sum, 1)
                    elif ph.name == "up":
                        j = t * 2 + n
                        total(pair[n][:, :, :], both(rstd))
                        dve.wait_ge(evac_done, g + 1)
                        dve.scalar_tensor_tensor(pair[n][:, :, :], pair[n][:, :, :], 0.0, pair[n][:, :, :], ALU.max,
                                                 ALU.mult).then_inc(hid_f, 1)
                        dve.wait_ge(hid_hi, c * 8 + j + 1)
                        dve.tensor_tensor(m_hl[:, bass.ds(j * 2, 2), 1, :], pair[n][:, :, :],
                                          m_hl[:, bass.ds(j * 2, 2), 0, :].bitcast(F32), ALU.subtract).then_inc(hid_lo, 1)
                    else:
                        j = t * 2 + n
                        r = res[:, bass.ds(j * 2, 2), :]
                        add_total(r)
                        if isinstance(c, int) and c == CHUNKS - 1:
                            finish_pair(j)
                if ph.name == "C" and t == PH["C"].trips - 1:
                    dve.memset(pair[2][:, :, :], 0.0).then_inc(r_sum, 1)

            def finish_pair(j):
                n = j % 2
                if j:
                    copy_y(j - 1)
                dve.wait_ge(y_sq, j + 1)
                src = (pair[2], gate)[n]
                if j == 0:
                    dve.tensor_copy(q_now[:, :, :], src[:, :, :]).then_inc(y_sum, 1)
                else:
                    dve.wait_ge(y_sum, j)
                    dve.tensor_tensor(q_now[:, :, :], q_now[:, :, :], src[:, :, :], ALU.add).then_inc(y_sum, 1)
                if j == NT // 2 - 1:
                    dve.wait_ge(y_sum, j + 1)
                    dve.tensor_tensor(stat[:, :], q_now[:, 0, :], q_now[:, 1, :], ALU.add).then_inc(fold3, 1)

            def copy_y(j):
                dve.wait_ge(y_t, j + 1)
                dve.tensor_copy(y_tok[:, :, 2 * j * P:(2 * j + 2) * P],
                                aux[j % 2][:, :].rearrange("p (b n) -> p b n", b=2)).then_inc(y_copied, 1)

            walk(dve, trip)
            copy_y(7)
            dve.wait_ge(stat3, 1)
            mean_eps(tok_stat[:, 0, :], aux[2][:, 0:2], 1.0 / D, RMS_EPS, var3)
            dve.wait_ge(root3, 1)
            dve.reciprocal(tok_stat[:, 2, :], tok_stat[:, 1, :]).then_inc(rstd3, 1)
            dve.wait_ge(rstd3, 1)
            dve.wait_ge(y_copied, 8)
            for i in range(2):
                dve.tensor_scalar(y_tok[:, 0, i * W2:(i + 1) * W2], y_tok[:, 0, i * W2:(i + 1) * W2],
                                  tok_stat[:, 2, 0:1], None, ALU.mult).then_inc(scaled[0], 1)

        @block.tensor
        def _(pe):
            def products(ph, c, t, k, act_hl):
                n, i, size = ph.slabs[k]
                s, g, q = slab_of(ph, c, t, k), group_of(ph, c, t, n), k % RING
                pe.wait_ge(lo_done, s + 1)
                if i == 0 and not (isinstance(g, int) and g < 2):
                    pe.wait_ge(evac_done, g - 1)
                b = bank(ph, n)
                for a in range(KT):
                    kt = i * KT + a
                    first, final = kt == 0, kt == size * KT - 1
                    for m in range(2):
                        w_h, w_l = (w[:, q, a, m * P:(m + 1) * P] for w in (w_hi, w_lo))
                        wide = (acc[:, b + m, :], w_h, act_hl[:, kt, :, :].rearrange("p h n -> p (h n)"))
                        narrow = (acc[:, b + m, 0:SEQ], w_l, act_hl[:, kt, 0, :])
                        if first:
                            pe.matmul(*wide, start=True, stop=False)
                            last = pe.matmul(*narrow, start=False, stop=False)
                        else:
                            pe.matmul(*narrow, start=False, stop=False)
                            last = pe.matmul(*wide, start=False, stop=final)
                last.then_inc(slab_used, 1)

            def transposed(dst, src):
                return pe.transpose(dst, src, ident[0:src.shape[0], 0:src.shape[0]])

            def sum_over_partitions(src_done, value, done):
                pe.wait_ge(src_done, value)
                pe.matmul(aux[2][:, 0:SEQ], ones[:, :], stat[:, :] if src_done is not fold1 else merged[:, 0, :],
                          start=True, stop=True).then_inc(done, 1)

            pe.wait_ge(consts, 2)
            pe.wait_ge(rows_g_in, 16)
            transposed(aux[3][:, PR_G1:PR_G1 + NT], rows_g[:, :]).then_inc(par_t, 1)
            def transpose_x(i):
                if i % 2 == 0:
                    pe.wait_ge(x_in[i // 2], 16)
                if i >= 3:
                    pe.wait_ge(x_copied, i - 2)
                for e in range(2):
                    for b in range(2):
                        last = transposed(aux[i % 3][:, e * SEQ + b * P:e * SEQ + (b + 1) * P],
                                          x_tok[:, b, (2 * i + e) * P:(2 * i + e + 1) * P])
                last.then_inc(x_t, 1)

            for i in range(6):
                transpose_x(i)

            def parameters():
                pe.wait_ge(rows_in, 8 * 16)
                transposed(aux[3][:, 0:PR_A], rows_a[:, :])
                transposed(aux[3][:, PR_LNG:PR_LNG + PR_B], rows_b[:, :])
                for j in range(HT):
                    at = PR_DW + j * TAPS
                    last = transposed(aux[3][:, at:at + TAPS], dw_rows[:, j * P:(j + 1) * P])
                last.then_inc(par_t, 1)

            def scores(t, p):
                if p == 0:
                    pe.wait_ge(q_ready, t * 2 + 2)
                    pe.wait_ge(v_ready, t * 2 + 2)
                else:
                    pe.wait_ge(masked, t * 4 + 2)
                for b, cols in ((0, slice(0, BLK)), (1, slice(BLK, SC))):
                    for e in range(2):
                        part = slice(e * HD, (e + 1) * HD)
                        last = pe.matmul(aux[e][:, cols], q_now[part, p, b * BLK:(b + 1) * BLK],
                                         k_now[part, 0, 0:(b + 1) * BLK],
                                         start=True, stop=True)
                last.then_inc(s_ready, 1)

            def transposes(t, p):
                pe.wait_ge(norm_step, t * 12 + 6 * p + 6)
                for e in range(2):
                    for b in range(3):
                        cols = slice(b * BLK, (b + 1) * BLK)
                        last = transposed(aux[2 + e][:, cols], probs[:, p, e, cols])
                last.then_inc(t_ready, 1)

            def values(t, p):
                pe.wait_ge(t_copied, t * 4 + 2 * p + 2)
                if p == 0:
                    pe.wait_ge(masked, t * 4 + 4)
                for e in range(2):
                    at = e * SEQ
                    pe.matmul(aux[p][:, at:at + BLK], v_now[:, 0, :], probs_t[:, e, 0:BLK], start=True, stop=True)
                    pe.matmul(aux[p][:, at + BLK:at + SEQ], v_now[:, 0, :], probs_t[:, e, BLK:2 * BLK], start=True, stop=False)
                    last = pe.matmul(aux[p][:, at + BLK:at + SEQ], v_now[:, 1, :], probs_t[:, e, 2 * BLK:], start=False, stop=True)
                last.then_inc(o_ready, 1)

            OPERAND = {"B": z_ba, "C": z_c, "A": z_ba, "mix": m_hl, "down": m_hl}

            def trip(ph, c, t):
                if ph == "v tokens":
                    pe.wait_ge(evac_done, PH["kv"].group0 + 2)
                    for b in range(2):
                        for e in range(2):
                            last = transposed(aux[2][:, b * KVW + e * P:b * KVW + (e + 1) * P],
                                              pair[1][:, e, b * P:(b + 1) * P])
                    last.then_inc(v_t, 1)
                    return
                for k in range(ph.nslabs):
                    n, i, size = ph.slabs[k]
                    operand = h_hl
                    if ph.name == "glu" and isinstance(t, int) and t == 0:
                        if n == 0:
                            pe.wait_ge(h_lo, KT * (i + 1))
                        if k == 1:
                            transpose_x(6)
                            transpose_x(7)
                        if k == 5:
                            sum_over_partitions(fold1, 8, stat1)
                            parameters()
                    if ph.name == "B":
                        for p in range(2):
                            if k == AT["scores"][p]:
                                scores(t, p)
                            if k == AT["transpose"][p]:
                                transposes(t, p)
                            if k == AT["values"][p]:
                                values(t, p)
                    if ph.name in ("B", "C", "A") and n % 2:
                        operand = OPERAND[ph.name]
                        if ph.name == "B":
                            pe.wait_ge(z_b_lo, 4)
                        elif ph.name == "C":
                            pe.wait_ge(o_step, 32)
                        else:
                            pe.wait_ge(ln_v, 31)
                    if ph.name == "C" and t * ph.nslabs + k == 28:
                        sum_over_partitions(ln_v, 4, ln_pe)
                    if ph.name == "C" and t * ph.nslabs + k == 36:
                        sum_over_partitions(ln_v, 11, ln_pe)
                    if ph.name == "mix":
                        operand = m_hl
                        pe.wait_ge(m_lo, 2 * (i + 1))
                    if ph.name == "up":
                        pe.wait_ge(r_lo, KT * (i + 1))
                        if isinstance(t, int) and t == 0 and k == 2:
                            sum_over_partitions(fold2, 1, stat2)
                    if ph.name == "down":
                        operand = m_hl
                        pe.wait_ge(hid_lo, c * 8 + 2 * (i + 1))
                        if isinstance(c, int) and c == CHUNKS - 1 and i == 2 and 2 * t + n >= 1:
                            transpose_y(2 * t + n - 1)
                    products(ph, c, t, k, operand)

            def transpose_y(j):
                pe.wait_ge(y_g, 2 * j + 2)
                if j >= 2:
                    pe.wait_ge(y_copied, j - 1)
                for e in range(2):
                    for b in range(2):
                        last = transposed(aux[j % 2][:, b * 2 * P + e * P:b * 2 * P + (e + 1) * P],
                                          pair[j % 2][:, e, b * P:(b + 1) * P])
                last.then_inc(y_t, 1)

            walk(pe, trip)
            transpose_y(7)
            pe.wait_ge(fold3, 1)
            for b in range(2):
                last = pe.matmul(aux[2][:, b:b + 1], stat[:, b * P:(b + 1) * P], ones[:, 0:1], start=True, stop=True)
            last.then_inc(stat3, 1)


_INS = ["x", "norm_mix_g", "w_in", "gate_b", "conf_dw", "conf_ln_g", "conf_ln_b", "w_conf_out", "sconv_w",
        "w_sconv_out", "sinks", "w_attn_out", "w_mix_out", "norm_ffn_g", "w_up", "w_down", "final_g"]


def kernel(**inputs):
    import numpy as np
    import concourse.bacc as bacc
    from concourse.bass_utils import run_bass_kernel_spmd

    nc = bacc.Bacc("TRN2", target_bir_lowering=False, num_devices=1)
    arrays, args = {}, []
    for name in _INS:
        a = np.ascontiguousarray(inputs[name])
        arrays[f"in_{name}"] = a
        args.append(nc.dram_tensor(f"in_{name}", a.shape, mybir.dt.from_np(a.dtype), kind="ExternalInput").ap())
    args.append(nc.dram_tensor("out_y", (1, SEQ, D), F32, kind="ExternalOutput").ap())
    build(nc, *args)
    r = run_bass_kernel_spmd(nc, [arrays], core_ids=[0])
    return r.results[0]["out_y"]
```
